# Optimizing a Trainium2 kernel written in Bass

```python
import jax, jax.numpy as jnp
from jax import lax
import numpy as np

D_MODEL = 1024
BATCH = 1
SEQ = 256
DEPTH = 2

CHUNK = 64
MEM_LEN = 256
Q_BLOCK = 128
N_MIXERS = 2
DA_HEADS = 6
DA_HEAD_DIM = 64
DA_WIDTH = DA_HEADS * 2 * DA_HEAD_DIM
HG_HEADS = 6
HG_KEY_DIM = 128
HG_VAL_DIM = 128
HG_KEY_WIDTH = HG_HEADS * HG_KEY_DIM
HG_VAL_WIDTH = HG_HEADS * HG_VAL_DIM
MEM_HEADS = 4
MEM_HEAD_DIM = 64
MEM_WIDTH = MEM_HEADS * MEM_HEAD_DIM
MIX_WIDTH = DA_WIDTH + MEM_WIDTH
D_FF_DENSE = 2816
N_EXPERTS = 8
TOP_K = 2
D_FF_EXPERT = 3584
EPS = 1e-6
MASK_VALUE = -1e30
N_A = (DEPTH + 1) // 2
N_B = DEPTH // 2


F32 = jnp.float32

def rms_norm(x, g):
    xf = x.astype(F32)
    y = xf * lax.rsqrt(jnp.mean(xf * xf, axis=-1, keepdims=True) + EPS)
    return (y * g.astype(F32)).astype(x.dtype)

def alibi_slopes(n):
    return jnp.asarray(2.0 ** (-8.0 * np.arange(1, n + 1) / n), F32)

def memory_attention(q_mem, mem, mem_norm_g, w_mem_kv):
    B, S, _ = q_mem.shape
    kv = rms_norm(mem, mem_norm_g) @ w_mem_kv
    k, v = jnp.split(kv, 2, axis=-1)
    q = q_mem.reshape(B, S, MEM_HEADS, MEM_HEAD_DIM)
    k = k.reshape(B, -1, MEM_HEADS, MEM_HEAD_DIM)
    v = v.reshape(B, -1, MEM_HEADS, MEM_HEAD_DIM)
    s = jnp.einsum('bshd,bmhd->bhsm', q, k).astype(F32) * (MEM_HEAD_DIM ** -0.5)
    p = jax.nn.softmax(s, axis=-1).astype(v.dtype)
    o = jnp.einsum('bhsm,bmhd->bshd', p, v)
    return o.reshape(B, S, MEM_WIDTH)

def diff_attention(q, k, v, lam, lam_init, subln_g):
    B, S = q.shape[:2]
    nb = S // Q_BLOCK
    scale = DA_HEAD_DIM ** -0.5
    slopes = alibi_slopes(DA_HEADS)
    kpos = jnp.arange(S)
    kchunk = kpos // CHUNK
    qb = q.reshape(B, nb, Q_BLOCK, DA_HEADS, 2, DA_HEAD_DIM).transpose(1, 0, 2, 3, 4, 5)
    starts = jnp.arange(nb) * Q_BLOCK

    def block(args):
        q_blk, start = args
        qpos = start + jnp.arange(Q_BLOCK)
        dist = jnp.abs(qpos[:, None] - kpos[None, :]).astype(F32)
        allowed = kchunk[None, :] <= (qpos // CHUNK)[:, None]
        bias = jnp.where(allowed[None], -slopes[:, None, None] * dist[None], MASK_VALUE)
        s = jnp.einsum('bqhmd,bkhmd->bhmqk', q_blk, k).astype(F32) * scale + bias[None, :, None]
        p = jax.nn.softmax(s, axis=-1)
        a = (p[:, :, 0] - lam * p[:, :, 1]).astype(v.dtype)
        return jnp.einsum('bhqk,bkhe->bqhe', a, v)

    o = lax.map(block, (qb, starts))
    o = o.transpose(1, 0, 2, 3, 4).reshape(B, S, DA_HEADS, 2 * DA_HEAD_DIM)
    o = rms_norm(o, subln_g) * (1.0 - lam_init)
    return o.reshape(B, S, DA_WIDTH)

def diff_attention_mixer(h, mem, w_in, lq1, lk1, lq2, lk2, subln_g, mem_norm_g, w_mem_kv, w_out, lam_init):
    B, S, _ = h.shape
    proj = h @ w_in
    q, k, v, qm = jnp.split(proj, [DA_WIDTH, 2 * DA_WIDTH, 3 * DA_WIDTH], axis=-1)
    q = q.reshape(B, S, DA_HEADS, 2, DA_HEAD_DIM)
    k = k.reshape(B, S, DA_HEADS, 2, DA_HEAD_DIM)
    v = v.reshape(B, S, DA_HEADS, 2 * DA_HEAD_DIM)
    lam = (jnp.exp(jnp.sum(lq1.astype(F32) * lk1.astype(F32)))
           - jnp.exp(jnp.sum(lq2.astype(F32) * lk2.astype(F32))) + lam_init)
    o = diff_attention(q, k, v, lam, lam_init, subln_g).astype(h.dtype)
    om = memory_attention(qm, mem, mem_norm_g, w_mem_kv).astype(h.dtype)
    return jnp.concatenate([o, om], axis=-1) @ w_out

def hgrn2_chunkwise(q, k, v, log_f):
    B, S, H, dk = q.shape
    dv = v.shape[-1]
    nc = S // CHUNK

    def to_chunks(t):
        return t.astype(F32).reshape(B, nc, CHUNK, H, t.shape[-1]).transpose(1, 0, 3, 2, 4)

    xs = (to_chunks(q), to_chunks(k), to_chunks(v), to_chunks(log_f))
    causal = jnp.tril(jnp.ones((CHUNK, CHUNK), bool))[None, None, :, :, None]

    def step(state, inp):
        q_, k_, v_, g_ = inp
        b = jnp.cumsum(g_, axis=2)
        b_last = b[:, :, -1:, :]
        diff = jnp.where(causal, b[:, :, :, None, :] - b[:, :, None, :, :], 0.0)
        decay = jnp.where(causal, jnp.exp(diff), 0.0)
        attn = jnp.einsum('bhtsk,bhsk->bhts', q_[:, :, :, None, :] * decay, k_)
        o = (jnp.einsum('bhts,bhsv->bhtv', attn, v_)
             + jnp.einsum('bhtk,bhkv->bhtv', q_ * jnp.exp(b), state))
        state = (jnp.exp(b_last)[:, :, 0, :, None] * state
                 + jnp.einsum('bhsk,bhsv->bhkv', k_ * jnp.exp(b_last - b), v_))
        return state, o

    state0 = jnp.zeros((B, H, dk, dv), F32)
    _, o = lax.scan(step, state0, xs)
    return o.transpose(1, 0, 3, 2, 4).reshape(B, S, H, dv)

def hgrn2_mixer(h, mem, w_in, lb, out_norm_g, mem_norm_g, w_mem_kv, w_out):
    B, S, _ = h.shape
    proj = h @ w_in
    q, fz, i, g, qm = jnp.split(
        proj, [HG_KEY_WIDTH, 2 * HG_KEY_WIDTH, 2 * HG_KEY_WIDTH + HG_VAL_WIDTH,
               2 * HG_KEY_WIDTH + 2 * HG_VAL_WIDTH], axis=-1)
    fz32 = fz.astype(F32)
    f = lb + (1.0 - lb) * jax.nn.sigmoid(fz32)
    log_f = jnp.log(f)
    k = (1.0 - lb) * jax.nn.sigmoid(-fz32)
    heads = lambda t: t.reshape(B, S, HG_HEADS, -1)
    o = hgrn2_chunkwise(heads(q), heads(k), heads(i), heads(log_f))
    o = rms_norm(o, out_norm_g) * jax.nn.silu(heads(g).astype(F32))
    o = o.reshape(B, S, HG_VAL_WIDTH).astype(h.dtype)
    om = memory_attention(qm, mem, mem_norm_g, w_mem_kv).astype(h.dtype)
    return jnp.concatenate([o, om], axis=-1) @ w_out

def dense_swiglu(h, w_gate_up, w_down):
    gt, up = jnp.split(h @ w_gate_up, 2, axis=-1)
    return (jax.nn.silu(gt) * up) @ w_down

def moe_swiglu(h, w_router, w_gate_up, w_down):
    B, S, D = h.shape
    t = h.reshape(-1, D)
    logits = (t @ w_router).astype(F32)
    top_val, top_idx = lax.top_k(logits, TOP_K)
    top_w = jax.nn.softmax(top_val, axis=-1)
    combine = jnp.sum(jax.nn.one_hot(top_idx, N_EXPERTS, dtype=F32) * top_w[..., None], axis=1)
    out = jnp.zeros_like(t)
    for e in range(N_EXPERTS):
        gt, up = jnp.split(t @ w_gate_up[e], 2, axis=-1)
        y = (jax.nn.silu(gt) * up) @ w_down[e]
        out = out + combine[:, e:e + 1].astype(t.dtype) * y
    return out.reshape(B, S, D)

def first_inputs(seed: int = 0) -> dict:
    key = jax.random.key(seed)
    ks = iter(jax.random.split(key, 40))
    D = D_MODEL
    res = (2.0 * DEPTH) ** -0.5

    def nrm(shape, scale):
        return jax.random.normal(next(ks), shape, F32) * scale

    def gain(shape):
        return 1.0 + 0.02 * jax.random.normal(next(ks), shape, F32)

    return {
        "x": nrm((BATCH, SEQ, D), 1.0),
        "mem": nrm((BATCH, MEM_LEN, D), 1.0),
        "a_norm_mix": gain((N_A, D)),
        "a_w_in": nrm((N_A, D, 3 * DA_WIDTH + MEM_WIDTH), D ** -0.5),
        "a_lam_q1": nrm((N_A, DA_HEAD_DIM), 0.1),
        "a_lam_k1": nrm((N_A, DA_HEAD_DIM), 0.1),
        "a_lam_q2": nrm((N_A, DA_HEAD_DIM), 0.1),
        "a_lam_k2": nrm((N_A, DA_HEAD_DIM), 0.1),
        "a_subln": gain((N_A, 2 * DA_HEAD_DIM)),
        "a_mem_norm": gain((N_A, D)),
        "a_w_mem_kv": nrm((N_A, D, 2 * MEM_WIDTH), D ** -0.5),
        "a_w_out": nrm((N_A, MIX_WIDTH, D), MIX_WIDTH ** -0.5 * res),
        "b_norm_mix": gain((N_B, D)),
        "b_w_in": nrm((N_B, D, 2 * HG_KEY_WIDTH + 2 * HG_VAL_WIDTH + MEM_WIDTH), D ** -0.5),
        "b_lb_logits": nrm((N_B, HG_KEY_WIDTH), 0.5),
        "b_out_norm": gain((N_B, HG_VAL_DIM)),
        "b_mem_norm": gain((N_B, D)),
        "b_w_mem_kv": nrm((N_B, D, 2 * MEM_WIDTH), D ** -0.5),
        "b_w_out": nrm((N_B, HG_VAL_WIDTH + MEM_WIDTH, D), (HG_VAL_WIDTH + MEM_WIDTH) ** -0.5 * res),
        "dense_norm": gain((N_A, D)),
        "dense_w_gate_up": nrm((N_A, D, 2 * D_FF_DENSE), D ** -0.5),
        "dense_w_down": nrm((N_A, D_FF_DENSE, D), D_FF_DENSE ** -0.5 * res),
        "moe_norm": gain((N_B, D)),
        "moe_router": nrm((N_B, D, N_EXPERTS), D ** -0.5),
        "moe_w_gate_up": nrm((N_B, N_EXPERTS, D, 2 * D_FF_EXPERT), D ** -0.5),
        "moe_w_down": nrm((N_B, N_EXPERTS, D_FF_EXPERT, D), D_FF_EXPERT ** -0.5 * res),
        "final_norm": gain((D,)),
    }

def first_block(x, mem,
              a_norm_mix, a_w_in, a_lam_q1, a_lam_k1, a_lam_q2, a_lam_k2, a_subln, a_mem_norm, a_w_mem_kv, a_w_out,
              b_norm_mix, b_w_in, b_lb_logits, b_out_norm, b_mem_norm, b_w_mem_kv, b_w_out,
              dense_norm, dense_w_gate_up, dense_w_down,
              moe_norm, moe_router, moe_w_gate_up, moe_w_down,
              final_norm):
    lb_p = jax.nn.softmax(b_lb_logits.astype(F32), axis=0)
    lb_all = jnp.cumsum(lb_p, axis=0) - lb_p[0:1]
    for i in range(DEPTH):
        if i % N_MIXERS == 0:
            j = i // N_MIXERS
            lam_init = 0.8 - 0.6 * float(np.exp(-0.3 * i))
            h = rms_norm(x, a_norm_mix[j])
            x = x + diff_attention_mixer(h, mem, a_w_in[j], a_lam_q1[j], a_lam_k1[j], a_lam_q2[j], a_lam_k2[j],
                                         a_subln[j], a_mem_norm[j], a_w_mem_kv[j], a_w_out[j], lam_init)
        else:
            j = i // N_MIXERS
            h = rms_norm(x, b_norm_mix[j])
            x = x + hgrn2_mixer(h, mem, b_w_in[j], lb_all[j], b_out_norm[j], b_mem_norm[j],
                                b_w_mem_kv[j], b_w_out[j])
        if i % 2 == 0:
            j = i // 2
            x = x + dense_swiglu(rms_norm(x, dense_norm[j]), dense_w_gate_up[j], dense_w_down[j])
        else:
            j = i // 2
            x = x + moe_swiglu(rms_norm(x, moe_norm[j]), moe_router[j], moe_w_gate_up[j], moe_w_down[j])
    return rms_norm(x, final_norm)


HEAD_DIM = 64
N_ATTN_HEADS = 8
N_KV_GROUPS = 2
GQA_RATIO = N_ATTN_HEADS // N_KV_GROUPS
ATTN_WIDTH = N_ATTN_HEADS * HEAD_DIM
N_MLP_GROUPS = 8
MLP_WIDTH = N_MLP_GROUPS * HEAD_DIM
MIX_WIDTH_2 = ATTN_WIDTH + MLP_WIDTH
KV_WIDTH = N_KV_GROUPS * HEAD_DIM
N_BRANCH = 3
GATE_WIDTH = N_ATTN_HEADS * N_BRANCH
IN_SIZES = [ATTN_WIDTH] + [KV_WIDTH] * 6 + [GATE_WIDTH, MLP_WIDTH, MLP_WIDTH]
IN_WIDTH = ATTN_WIDTH + 6 * KV_WIDTH + GATE_WIDTH + 2 * MLP_WIDTH
ROT_DIM = HEAD_DIM // 4
ROPE_THETA = 500000.0
CMP_LEN = 32
CMP_STRIDE = 16
CMP_HIDDEN = 256
SEL_LEN = 64
N_SELECT = 16
WINDOW = 512
CHUNK_2 = 128
D_FF = 2816
CONV_WIDTH = 3
PLE_DIM = 256
NORM_EPS = 1e-6
NEG = -1e30
FORCED = 1e9


def rms_norm_2(x, gain):
    xf = x.astype(jnp.float32)
    y = xf * lax.rsqrt(jnp.mean(xf * xf, axis=-1, keepdims=True) + NORM_EPS)
    return (y * gain.astype(jnp.float32)).astype(x.dtype)

def layer_norm(x, gain, bias):
    xf = x.astype(jnp.float32)
    mu = jnp.mean(xf, axis=-1, keepdims=True)
    var = jnp.mean(jnp.square(xf - mu), axis=-1, keepdims=True)
    y = (xf - mu) * lax.rsqrt(var + NORM_EPS) * gain.astype(jnp.float32) + bias.astype(jnp.float32)
    return y.astype(x.dtype)

def rope_partial(x, pos):
    half = ROT_DIM // 2
    inv = ROPE_THETA ** (-jnp.arange(half, dtype=jnp.float32) / half)
    ang = pos.astype(jnp.float32)[:, None] * inv[None, :]
    cos = jnp.cos(ang)[:, None, :]
    sin = jnp.sin(ang)[:, None, :]
    xr = x[..., :ROT_DIM].astype(jnp.float32)
    x1, x2 = xr[..., :half], xr[..., half:]
    rot = jnp.concatenate([x1 * cos - x2 * sin, x2 * cos + x1 * sin], axis=-1).astype(x.dtype)
    return jnp.concatenate([rot, x[..., ROT_DIM:]], axis=-1)

def masked_softmax(s, mask):
    s = jnp.where(mask, s, NEG)
    m = jnp.max(s, axis=-1, keepdims=True)
    e = jnp.exp(s - m) * mask
    return e / jnp.maximum(jnp.sum(e, axis=-1, keepdims=True), 1e-30)

def compress(t, pe, w1, b1, w2, b2):
    B, S, G, D = t.shape
    r = CMP_LEN // CMP_STRIDE
    nch = S // CMP_STRIDE
    nc = nch - r + 1
    ch = t.reshape(B, nch, CMP_STRIDE, G, D)
    blocks = jnp.concatenate([ch[:, j:j + nc] for j in range(r)], axis=2)
    blocks = blocks + pe[None, None, :, None, :]
    flat = blocks.transpose(0, 1, 3, 2, 4).reshape(B, nc, G, CMP_LEN * D)
    h = jax.nn.gelu(flat @ w1 + b1)
    return h @ w2 + b2

def nsa_attention(q, kc, vc, ks, vs, kw, vw, gates):
    B, S, H, D = q.shape
    G = kc.shape[2]
    R = H // G
    nc = kc.shape[1]
    ns = S // SEL_LEN
    n_sel = min(N_SELECT, ns)
    scale = D ** -0.5
    cmp_start = jnp.arange(nc) * CMP_STRIDE
    cmp_end = cmp_start + CMP_LEN - 1
    sel_start = jnp.arange(ns) * SEL_LEN
    overlap = ((cmp_end[:, None] >= sel_start[None, :]) &
               (cmp_start[:, None] <= sel_start[None, :] + SEL_LEN - 1)).astype(jnp.float32)
    ks_blk = ks.reshape(B, ns, SEL_LEN, G, D).transpose(0, 3, 1, 2, 4)
    vs_blk = vs.reshape(B, ns, SEL_LEN, G, D).transpose(0, 3, 1, 2, 4)
    kw_pad = jnp.pad(kw, ((0, 0), (WINDOW, 0), (0, 0), (0, 0)))
    vw_pad = jnp.pad(vw, ((0, 0), (WINDOW, 0), (0, 0), (0, 0)))
    qg = q.reshape(B, S, G, R, D)
    gg = gates.reshape(B, S, G, R, N_BRANCH)
    bi = jnp.arange(B)[:, None, None, None]
    gi = jnp.arange(G)[None, :, None, None]
    blk = jnp.arange(ns)
    f32 = jnp.float32

    def block(qi):
        t0 = qi * Q_BLOCK
        tq = t0 + jnp.arange(Q_BLOCK)
        qb = lax.dynamic_slice_in_dim(qg, t0, Q_BLOCK, axis=1)
        gb = lax.dynamic_slice_in_dim(gg, t0, Q_BLOCK, axis=1)
        s_c = jnp.einsum('bqgrd,bngd->bgrqn', qb, kc, preferred_element_type=f32) * scale
        p_c = masked_softmax(s_c, cmp_end[None, :] <= tq[:, None])
        o_c = jnp.einsum('bgrqn,bngd->bqgrd', p_c.astype(vc.dtype), vc)
        imp = jnp.einsum('bgrqn,nj->bgqj', p_c, overlap)
        cur = tq // SEL_LEN
        valid = blk[None, :] <= cur[:, None]
        forced = valid & ((blk[None, :] == 0) | (blk[None, :] == cur[:, None]) | (blk[None, :] == cur[:, None] - 1))
        score = jnp.where(forced, FORCED, jnp.where(valid, imp, NEG))
        vals, idx = lax.top_k(score, n_sel)
        sel_ok = vals > NEG * 0.5
        k_g = ks_blk[bi, gi, idx].reshape(B, G, Q_BLOCK, n_sel * SEL_LEN, D)
        v_g = vs_blk[bi, gi, idx].reshape(B, G, Q_BLOCK, n_sel * SEL_LEN, D)
        kpos = idx[..., None] * SEL_LEN + jnp.arange(SEL_LEN)
        mask_s = ((kpos <= tq[:, None, None]) & sel_ok[..., None]).reshape(B, G, Q_BLOCK, n_sel * SEL_LEN)
        s_s = jnp.einsum('bqgrd,bgqkd->bgrqk', qb, k_g, preferred_element_type=f32) * scale
        p_s = masked_softmax(s_s, mask_s[:, :, None])
        o_s = jnp.einsum('bgrqk,bgqkd->bqgrd', p_s.astype(v_g.dtype), v_g)
        kwb = lax.dynamic_slice_in_dim(kw_pad, t0, Q_BLOCK + WINDOW, axis=1)
        vwb = lax.dynamic_slice_in_dim(vw_pad, t0, Q_BLOCK + WINDOW, axis=1)
        kpos_w = t0 - WINDOW + jnp.arange(Q_BLOCK + WINDOW)
        mask_w = ((kpos_w[None, :] <= tq[:, None]) & (kpos_w[None, :] > tq[:, None] - WINDOW)
                  & (kpos_w[None, :] >= 0))
        s_w = jnp.einsum('bqgrd,bkgd->bgrqk', qb, kwb, preferred_element_type=f32) * scale
        p_w = masked_softmax(s_w, mask_w)
        o_w = jnp.einsum('bgrqk,bkgd->bqgrd', p_w.astype(vwb.dtype), vwb)
        o = gb[..., 0:1] * o_c + gb[..., 1:2] * o_s + gb[..., 2:3] * o_w
        return o.reshape(B, Q_BLOCK, H * D)

    out = lax.map(block, jnp.arange(S // Q_BLOCK))
    return out.transpose(1, 0, 2, 3).reshape(B, S, H * D)

def spatial_gating(u, v, ln_g, ln_b, w_s, b_s):
    B, S, _ = u.shape
    u = jax.nn.gelu(u)
    v = layer_norm(jax.nn.gelu(v), ln_g, ln_b)
    vc = v.reshape(B, S // CHUNK_2, CHUNK_2, N_MLP_GROUPS, HEAD_DIM)
    causal = jnp.tril(jnp.ones((CHUNK_2, CHUNK_2), dtype=bool))
    ws = jnp.where(causal[None], w_s, 0)
    mixed = jnp.einsum('gts,bcsgd->bctgd', ws, vc) + b_s.T[None, None, :, :, None]
    return u * mixed.reshape(B, S, MLP_WIDTH)

def conv_ffn(x, w_up, conv_w, conv_b, w_down):
    S = x.shape[1]
    h = x @ w_up
    hp = jnp.pad(h, ((0, 0), (CONV_WIDTH - 1, 0), (0, 0)))
    hc = conv_b
    for k in range(CONV_WIDTH):
        hc = hc + hp[:, k:k + S] * conv_w[k]
    g, up = jnp.split(hc, 2, axis=-1)
    return (jax.nn.silu(g) * up) @ w_down

def second_inputs(seed: int = 0) -> dict:
    key = jax.random.key(seed)
    ks = jax.random.split(key, 32)
    L = DEPTH

    def nrm(k, shape, scale):
        return jax.random.normal(k, shape, dtype=jnp.float32) * scale

    def gain(k, shape):
        return 1.0 + nrm(k, shape, 0.05)

    return {
        "x": nrm(ks[0], (BATCH, SEQ, D_MODEL), 1.0),
        "p": nrm(ks[1], (DEPTH, BATCH, SEQ, PLE_DIM), 1.0),
        "pre_mix_g": gain(ks[2], (L, D_MODEL)),
        "w_in": nrm(ks[3], (L, D_MODEL, IN_WIDTH), D_MODEL ** -0.5),
        "cmp_pe": nrm(ks[4], (L, 2, CMP_LEN, HEAD_DIM), 0.1),
        "cmp_w1": nrm(ks[5], (L, 2, CMP_LEN * HEAD_DIM, CMP_HIDDEN), (CMP_LEN * HEAD_DIM) ** -0.5),
        "cmp_b1": nrm(ks[6], (L, 2, CMP_HIDDEN), 0.02),
        "cmp_w2": nrm(ks[7], (L, 2, CMP_HIDDEN, HEAD_DIM), CMP_HIDDEN ** -0.5),
        "cmp_b2": nrm(ks[8], (L, 2, HEAD_DIM), 0.02),
        "gmlp_ln_g": gain(ks[9], (L, MLP_WIDTH)),
        "gmlp_ln_b": nrm(ks[10], (L, MLP_WIDTH), 0.02),
        "gmlp_ws": nrm(ks[11], (L, N_MLP_GROUPS, CHUNK_2, CHUNK_2), 0.5 * CHUNK_2 ** -0.5),
        "gmlp_bs": 1.0 + nrm(ks[12], (L, N_MLP_GROUPS, CHUNK_2), 0.1),
        "attn_out_g": gain(ks[13], (L, ATTN_WIDTH)),
        "mlp_out_g": gain(ks[14], (L, MLP_WIDTH)),
        "w_o": nrm(ks[15], (L, MIX_WIDTH_2, D_MODEL), MIX_WIDTH_2 ** -0.5),
        "post_mix_g": gain(ks[16], (L, D_MODEL)),
        "pre_ffn_g": gain(ks[17], (L, D_MODEL)),
        "w_up": nrm(ks[18], (L, D_MODEL, 2 * D_FF), D_MODEL ** -0.5),
        "conv_w": nrm(ks[19], (L, CONV_WIDTH, 2 * D_FF), CONV_WIDTH ** -0.5),
        "conv_b": nrm(ks[20], (L, 2 * D_FF), 0.02),
        "w_down": nrm(ks[21], (L, D_FF, D_MODEL), D_FF ** -0.5),
        "post_ffn_g": gain(ks[22], (L, D_MODEL)),
        "ple_norm_g": gain(ks[23], (L, D_MODEL)),
        "w_ple_gate": nrm(ks[24], (L, D_MODEL, D_MODEL), D_MODEL ** -0.5),
        "w_ple_proj": nrm(ks[25], (L, PLE_DIM, D_MODEL), PLE_DIM ** -0.5),
    }

def second_block(x, p, pre_mix_g, w_in, cmp_pe, cmp_w1, cmp_b1, cmp_w2, cmp_b2,
              gmlp_ln_g, gmlp_ln_b, gmlp_ws, gmlp_bs, attn_out_g, mlp_out_g, w_o,
              post_mix_g, pre_ffn_g, w_up, conv_w, conv_b, w_down, post_ffn_g,
              ple_norm_g, w_ple_gate, w_ple_proj):
    B, S, _ = x.shape
    pos = jnp.arange(S)
    split_at = [int(o) for o in np.cumsum(IN_SIZES)[:-1]]
    nc = S // CMP_STRIDE - CMP_LEN // CMP_STRIDE + 1
    cmp_pos = jnp.arange(nc) * CMP_STRIDE + CMP_LEN - 1
    h = x
    for i in range(DEPTH):
        a = rms_norm_2(h, pre_mix_g[i])
        z = a @ w_in[i]
        zq, zkc, zvc, zks, zvs, zkw, zvw, zg, zu, zv = jnp.split(z, split_at, axis=-1)
        kv = lambda t: t.reshape(B, S, N_KV_GROUPS, HEAD_DIM)
        q = rope_partial(zq.reshape(B, S, N_ATTN_HEADS, HEAD_DIM), pos)
        kc = compress(kv(zkc), cmp_pe[i, 0], cmp_w1[i, 0], cmp_b1[i, 0], cmp_w2[i, 0], cmp_b2[i, 0])
        vc = compress(kv(zvc), cmp_pe[i, 1], cmp_w1[i, 1], cmp_b1[i, 1], cmp_w2[i, 1], cmp_b2[i, 1])
        kc = rope_partial(kc, cmp_pos)
        k_sel = rope_partial(kv(zks), pos)
        k_win = rope_partial(kv(zkw), pos)
        gates = jax.nn.sigmoid(zg.reshape(B, S, N_ATTN_HEADS, N_BRANCH))
        attn = nsa_attention(q, kc, vc, k_sel, kv(zvs), k_win, kv(zvw), gates)
        mlp = spatial_gating(zu, zv, gmlp_ln_g[i], gmlp_ln_b[i], gmlp_ws[i], gmlp_bs[i])
        mix = jnp.concatenate([rms_norm_2(attn, attn_out_g[i]), rms_norm_2(mlp, mlp_out_g[i])], axis=-1) @ w_o[i]
        h = h + rms_norm_2(mix, post_mix_g[i])
        f = conv_ffn(rms_norm_2(h, pre_ffn_g[i]), w_up[i], conv_w[i], conv_b[i], w_down[i])
        h = h + rms_norm_2(f, post_ffn_g[i])
        gate = jax.nn.sigmoid(rms_norm_2(h, ple_norm_g[i]) @ w_ple_gate[i])
        h = h + gate * (p[i] @ w_ple_proj[i])
    return h


def setup_inputs(seed=0):
    out = dict(first_inputs(seed))
    for name, value in second_inputs(seed + 1).items():
        if name != "x":
            out[name + "_2"] = value
    return out


def reference(
    x, mem, a_norm_mix, a_w_in, a_lam_q1, a_lam_k1, a_lam_q2, a_lam_k2, a_subln, a_mem_norm,
    a_w_mem_kv, a_w_out, b_norm_mix, b_w_in, b_lb_logits, b_out_norm, b_mem_norm, b_w_mem_kv,
    b_w_out, dense_norm, dense_w_gate_up, dense_w_down, moe_norm, moe_router, moe_w_gate_up,
    moe_w_down, final_norm, p_2, pre_mix_g_2, w_in_2, cmp_pe_2, cmp_w1_2, cmp_b1_2, cmp_w2_2,
    cmp_b2_2, gmlp_ln_g_2, gmlp_ln_b_2, gmlp_ws_2, gmlp_bs_2, attn_out_g_2, mlp_out_g_2, w_o_2,
    post_mix_g_2, pre_ffn_g_2, w_up_2, conv_w_2, conv_b_2, w_down_2, post_ffn_g_2, ple_norm_g_2,
    w_ple_gate_2, w_ple_proj_2,
):
    x = first_block(
        x, mem, a_norm_mix, a_w_in, a_lam_q1, a_lam_k1, a_lam_q2, a_lam_k2, a_subln, a_mem_norm,
        a_w_mem_kv, a_w_out, b_norm_mix, b_w_in, b_lb_logits, b_out_norm, b_mem_norm,
        b_w_mem_kv, b_w_out, dense_norm, dense_w_gate_up, dense_w_down, moe_norm, moe_router,
        moe_w_gate_up, moe_w_down, final_norm,
    )
    return second_block(
        x, p_2, pre_mix_g_2, w_in_2, cmp_pe_2, cmp_w1_2, cmp_b1_2, cmp_w2_2, cmp_b2_2,
        gmlp_ln_g_2, gmlp_ln_b_2, gmlp_ws_2, gmlp_bs_2, attn_out_g_2, mlp_out_g_2, w_o_2,
        post_mix_g_2, pre_ffn_g_2, w_up_2, conv_w_2, conv_b_2, w_down_2, post_ffn_g_2,
        ple_norm_g_2, w_ple_gate_2, w_ple_proj_2,
    )


_drawn_inputs = setup_inputs


def setup_inputs(seed=0):
    import zlib

    import numpy as np

    out = dict(_drawn_inputs(seed))
    spreads = {}
    factors = {'a_lam_q2': 2.778,
     'a_subln': 4.889,
     'a_mem_norm': 8.0,
     'b_norm_mix': 3.702,
     'b_out_norm': 7.601,
     'b_mem_norm': 8.0,
     'dense_norm': 3.977,
     'cmp_b1_2': 3.639,
     'gmlp_ln_g_2': 4.85,
     'gmlp_ln_b_2': 22.62,
     'ple_norm_g_2': 7.289,
     'moe_norm': 8.0}
    for name, (base, spread) in spreads.items():
        noise = np.random.default_rng([zlib.crc32(name.encode()), seed]).standard_normal(out[name].shape)
        drawn = base * np.exp(spread * noise) if base else spread * noise
        out[name] = __import__('jax').numpy.asarray(drawn.astype(out[name].dtype))
    for name, factor in factors.items():
        out[name] = (out[name] * factor).astype(out[name].dtype)
    return out
```

```python
import numpy as np
import concourse.bass as bass
from concourse import mybir
from concourse.alu_op_type import AluOpType as ALU

F32 = mybir.dt.float32
I32 = mybir.dt.int32
U32 = mybir.dt.uint32
ACT = mybir.ActivationFunctionType
AX_X = mybir.AxisListType.X

P = 128
S = 256
TT = S // P
D = 1024
KT = D // P
EPS = 1e-6
NEG = -1e30
FAR = 1e32

HEADS = 6
MEM_HEADS = 4
HD = 64
CH = 64
LAM_INIT = 0.8 - 0.6 * float(np.exp(-0.3 * 0))
SLOPES = [float(np.float32(2.0 ** (-8.0 * (h + 1) / HEADS))) for h in range(HEADS)]

FF = 2816
FE = 3584
NE = 8
TURN = 7

NH2 = 8
GROUPS = 2
NC = 15
CSTR = 16
PAIRS = 16
GW = 24
FFCOLS = 2 * D + D
SLOT = FFCOLS + 8


class Line:

    def __init__(self, nc, name, eng=None, step=1):
        self.nc, self.eng, self.step = nc, eng, step
        self.sem = nc.alloc_semaphore(name)
        self.reset()

    def reset(self):
        self.count, self.turn, self.start, self.seen = 0, 0, 0, {}

    def wait(self, *marks):
        for line, value, turn in marks:
            key = (line, turn)
            if self.seen.get(key, 0) >= value:
                continue
            self.seen[key] = value
            self.eng.wait_ge(line.sem, line.index * turn + value if turn else value)

    def mark(self, inst):
        inst.then_inc(self.sem, self.step)
        self.count += self.step
        return (self, self.count, self.turn)

    def __call__(self, marks, fn, *args, **kw):
        self.wait(*marks)
        return self.mark(fn(*args, **kw))

    def now(self):
        return (self, self.count, self.turn)


class Turns:

    def __init__(self, nc, n, lines, per_turn):
        self.nc, self.n, self.lines, self.per = nc, n, lines, per_turn
        self.fori = nc.Fori(0, n)

    def __enter__(self):
        i = self.fori.__enter__()
        for q in self.lines:
            q.index, q.start, q.turn, q.seen = i, q.count, self.per[q], {}
        return i

    def __exit__(self, *exc):
        for q in self.lines:
            if exc[0] is None:
                assert q.count - q.start == q.turn, (q.sem.name, q.count - q.start, q.turn)
            q.count = q.start + self.n * q.turn
            q.turn, q.seen = 0, {}
        return self.fori.__exit__(*exc)


def before(mark):
    line, value, turn = mark
    assert value - turn > 0, (line.sem.name, value, turn)
    return (line, value - turn, turn)


class Bank:

    def __init__(self, ap):
        self.ap, self.free = ap, ()


class Ring:

    def __init__(self, nc, sp, W, lines):
        self.nc, self.sp, self.W, self.lines = nc, sp, W, lines
        self.reset()

    def reset(self):
        self.free = [() for _ in self.lines]
        self.sources, self.loaded, self.taken, self.given = [], 0, 0, 0

    def plan(self, sources):
        self.sources += sources
        self._fill()

    def _fill(self):
        while self.loaded < len(self.sources) and self.loaded < self.given + len(self.lines):
            k = self.loaded % len(self.lines)
            src = self.sources[self.loaded]
            n = src.shape[-1]
            self.sp.wait(*self.free[k])
            self.lines[k].mark(self.nc.sync.dma_start(self.W[:, k, 0:n], src))
            self.loaded += 1

    def take(self):
        k = self.taken % len(self.lines)
        self.taken += 1
        return k, self.W[:, k, :], self.lines[k].now()

    def give(self, k, mark):
        self.free[k] = (mark,)
        self.given += 1
        self._fill()


def program(nc, dr, out):
    vec, act_e, pe_e, pool_e, sync = nc.vector, nc.scalar, nc.tensor, nc.gpsimd, nc.sync
    V = Line(nc, "vector_done", vec)
    A = Line(nc, "scalar_done", act_e)
    T = Line(nc, "tensor_done", pe_e)
    G = Line(nc, "gpsimd_done", pool_e)
    SP = Line(nc, "sync_done", sync)
    slots = [Line(nc, f"slot{k}_loaded", step=16) for k in range(TURN)]
    const_in = Line(nc, "constants_loaded", step=16)
    mem_in = Line(nc, "memory_loaded", step=16)
    layer_in = Line(nc, "layer_loaded", step=16)
    stored = Line(nc, "result_stored", step=16)
    lines = [V, A, T, G, SP, *slots, const_in, mem_in, layer_in]

    def sb(name, shape, dt=F32):
        return nc.alloc_sbuf_tensor(name, shape, dt)

    X = sb("residual", [P, TT, D])
    HT = sb("hidden_columns", [P, KT, S])
    XN = sb("normalised_rows", [P, TT, D])
    MT = sb("memory_columns", [P, KT, S])
    W = sb("weight_ring", [P, TURN, SLOT])
    AT = sb("gated_columns", [P, TURN, S])
    SG = sb("silu_columns", [P, 2, S])
    IDENT = sb("identity", [P, P])
    DIST = sb("distance", [P, 384])
    CAUS = sb("causal", [P, 384])
    LEVEL = sb("level_masks", [P, 8, P], I32)
    RESET = sb("chunk_reset", [P, S])
    TRIL = sb("keep_lower", [P, P])
    ROPE = sb("rope", [P, TT, 16])
    CROPE = sb("rope_compressed", [NC, 16])
    CMPA = sb("compressed_mask_add", [P, TT, NC])
    CMPK = sb("compressed_mask_keep", [P, TT, NC])
    IOTA = sb("expert_numbers", [P, NE])
    ONES = sb("ones", [P, P])
    GAINS = sb("gains", [P, 7, KT])
    SMALL = sb("small_parameters", [P, 10])
    LBL = sb("bound_logits", [P, HEADS])
    ROUT = sb("router", [P, KT, NE])
    FING = sb("row_gain", [P, D])
    ST = sb("statistics", [P, 160])
    STI = sb("indices", [P, 16], U32)
    ARENA = sb("arena", [P, 14600])
    PS = nc.alloc_psum_tensor("banks", [P, 8, 512], F32)
    banks = [Bank(PS[:, b, :]) for b in range(8)]
    ring = Ring(nc, SP, W, slots)

    used = [0]

    def room(*shape):
        n = int(np.prod(shape))
        a, used[0] = used[0], used[0] + n
        assert used[0] <= 14600, used[0]
        ap = ARENA[:, a:a + n]
        if len(shape) == 2:
            ap = ap.rearrange("p (a b) -> p a b", a=shape[0])
        if len(shape) == 3:
            ap = ap.rearrange("p (a b c) -> p a b c", a=shape[0], b=shape[1])
        return ap

    stat_used = [0]

    def stat(n=1):
        if stat_used[0] + n > 160:
            stat_used[0] = 0
        a = stat_used[0]
        stat_used[0] += n
        return ST[:, a:a + n]

    def spread(ap, n):
        return ap.unsqueeze(2).broadcast_to([ap.shape[0], ap.shape[1], n])


    def root(ssq, n, width, ready):
        m = V(ready, vec.tensor_scalar, ssq, ssq, 1.0 / width, EPS, ALU.mult, ALU.add)
        m = A((m,), act_e.activation, ssq, ssq, ACT.Sqrt)
        return V((m,), vec.reciprocal, ssq, ssq)

    def turn(src, n, gain, dst, ready, free=()):
        marks, k = [], 0
        for t in range(TT):
            for c0 in range(0, n, 4):
                w = min(4, n - c0)
                bank = banks[4 + k % 4]
                k += 1
                T.wait(*ready, *bank.free)
                for c in range(w):
                    last = pe_e.transpose(bank.ap[:, c * P:(c + 1) * P], src(t, c0 + c), IDENT[:, :])
                turned = T.mark(last)
                seen = bank.ap[:, 0:w * P].rearrange("p (c t) -> p c t", c=w)
                to = dst[:, c0:c0 + w, t * P:(t + 1) * P]
                if gain is None:
                    m = A((turned, *free), act_e.copy, to, seen)
                else:
                    m = V((turned, *free), vec.tensor_tensor, to, seen, spread(gain[:, c0:c0 + w], P), ALU.mult)
                bank.free = (m,)
                marks.append(m)
        return tuple(marks[-4:])

    def rms_scale(src, dst, width, ready, free=()):
        ssq = stat(TT)
        marks = []
        for t in range(TT):
            marks.append(A((*ready, *free), act_e.activation, dst[:, t, :], src[:, t, :], ACT.Square,
                           accum_out=ssq[:, t:t + 1]))
        r = root(ssq, TT, width, tuple(marks))
        return tuple(A((r,), act_e.activation, dst[:, t, :], src[:, t, :], ACT.Copy, scale=ssq[:, t:t + 1])
                     for t in range(TT))

    def norm_columns(src, gain, dst, ready, free=()):
        m = rms_scale(src, XN, D, ready, (T.now(), V.now()))
        return turn(lambda t, c: XN[:, t, c * P:(c + 1) * P], KT, gain, dst, m, free)

    bank_turn = [0]

    def next_bank():
        bank_turn[0] += 1
        return banks[4 + bank_turn[0] % 4]

    def project(n, src, ready, evac, form, kt=KT):
        out_marks = []
        for c in range(n):
            k, w, arrived = ring.take()
            w = w[:, 0:kt * 256].rearrange("p (k n) -> p k n", k=kt)
            bank = next_bank()
            T.wait(arrived, *ready, *bank.free)
            for s in range(2):
                for i in range(kt):
                    cut = slice(s * P, (s + 1) * P)
                    if form == "rows":
                        lhs, rhs = src[:, i, cut], w[:, i, :]
                    else:
                        lhs, rhs = w[:, i, cut], src[:, i, :]
                    last = pe_e.matmul(bank.ap[:, s * 256:(s + 1) * 256], lhs, rhs, start=i == 0, stop=i == kt - 1)
            m = T.mark(last)
            ring.give(k, m)
            bank.free = evac(c, bank.ap.rearrange("p (s n) -> p s n", s=2), m)
            out_marks += bank.free
        return tuple(out_marks)

    def copy_to(dst, scale=1.0, func=ACT.Copy):
        def go(c, seen, m):
            return (A((m,), act_e.activation, dst[:, 2 * c:2 * c + 2, :], seen, func, scale=scale),)
        return go

    def copy_rows(dst, scale=1.0, func=ACT.Copy):
        def go(c, seen, m):
            return (A((m,), act_e.activation, dst[:, :, c * 256:(c + 1) * 256], seen, func, scale=scale),)
        return go

    def add_rows(dst):
        def go(c, seen, m):
            part = dst[:, :, c * 256:(c + 1) * 256]
            return (V((m,), vec.tensor_tensor, part, part, seen, ALU.add),)
        return go

    TRI = [(0, P, 0), (1, S, P)]
    FULL = [(0, S, 0), (1, S, S)]

    def attend(heads, segs, q_of, k_of, v_of, prepare, finish, ready, bufs, vw, keys=P, keep=None, maps=1):
        ncol = max(c + n for _, n, c in segs)
        P_, PT = bufs
        state = {}

        def scores(h):
            got = []
            for m in range(maps):
                bank = banks[(h * maps + m) % 4]
                T.wait(*ready, *bank.free)
                for q, n, c in segs:
                    last = pe_e.matmul(bank.ap[:, c:c + n], q_of(h, m, q), k_of(h, m, n), start=True, stop=True)
                got.append((bank, T.mark(last)))
            state[h] = got

        def soften(h):
            ps = P_[h % 2]
            res = []
            for m, (bank, made) in enumerate(state[h]):
                raw = bank.ap[:, 0:ncol]
                mine = ps[:, m, 0:ncol]
                free = state.get(("turned", h - 2), ())
                if prepare is None:
                    V.wait(made, *free)
                    ready_s, from_ = made, raw
                else:
                    ready_s = prepare(h, mine, raw, (made, *free))
                    from_ = mine
                top, tot = stat(2), stat(2)
                if segs == FULL:
                    mx = V((ready_s,), vec.tensor_reduce, top, from_.rearrange("p (s n) -> p s n", s=2), AX_X,
                           ALU.max, negate=True)
                else:
                    for i, (q, n, c) in enumerate(segs):
                        mx = V((ready_s,), vec.tensor_reduce, top[:, i:i + 1], from_[:, c:c + n], AX_X, ALU.max,
                               negate=True)
                for i, (q, n, c) in enumerate(segs):
                    e = A((mx, *free), act_e.activation, mine[:, c:c + n], from_[:, c:c + n], ACT.Exp,
                          bias=top[:, i:i + 1], accum_out=tot[:, i:i + 1])
                bank.free = (e, mx)
                res.append((tot, e))
            if maps == 2:
                (t0, e0), (t1, e1) = res
                r = V((e0, e1), vec.reciprocal, t0, t0)
                V((), vec.reciprocal, t1, t1)
                r = V((V.now(),), vec.tensor_scalar, t1, t1, LAM, None, ALU.mult)
                for i, (q, n, c) in enumerate(segs):
                    V((r,), vec.tensor_scalar, ps[:, 1, c:c + n], ps[:, 1, c:c + n], t1[:, i:i + 1], None, ALU.mult)
                sub = V.now()
                for i, (q, n, c) in enumerate(segs):
                    e = V((sub,), vec.scalar_tensor_tensor, ps[:, 0, c:c + n], ps[:, 0, c:c + n], t0[:, i:i + 1],
                          ps[:, 1, c:c + n], ALU.mult, ALU.subtract)
                state["p", h] = (None, e)
            else:
                tot, e = res[0]
                if keep is not None:
                    e = V((e,), vec.tensor_tensor, ps[:, 0, 0:ncol], ps[:, 0, 0:ncol], keep, ALU.mult)
                    e = V((e,), vec.tensor_reduce, tot, ps[:, 0, 0:ncol].rearrange("p (s n) -> p s n", s=2), AX_X,
                          ALU.add)
                    e = V((e,), vec.tensor_scalar, tot, tot, 1e-30, None, ALU.max)
                e = V((e,), vec.reciprocal, tot, tot)
                state["p", h] = (tot, e)

        def turn_p(h):
            tot, e = state["p", h]
            ps, pt = P_[h % 2], PT[h % 2]
            bank = banks[4 + h % 2]
            T.wait(e, *bank.free)
            col = 0
            for q, n, c in segs:
                for k0 in range(0, n, keys):
                    last = pe_e.transpose(bank.ap[0:keys, col:col + P], ps[:, 0, c + k0:c + k0 + keys], IDENT[:, :])
                    col += P
            m = T.mark(last)
            state["turned", h] = (m,)
            cp = V if h % 2 else A
            fn = vec.tensor_copy if h % 2 else act_e.copy
            got = cp((m, *state.get(("used", h - 2), ())), fn, pt[0:keys, 0:col], bank.ap[0:keys, 0:col])
            bank.free = (got,)
            state["pt", h] = got

        def values(h):
            tot, _ = state["p", h]
            pt = PT[h % 2]
            bank = banks[6 + h % 2]
            T.wait(state["pt", h], *bank.free)
            col = 0
            for q, n, c in segs:
                kts = range(0, n, keys)
                for i in kts:
                    last = pe_e.matmul(bank.ap[:, q * vw:(q + 1) * vw], pt[0:keys, col:col + P], v_of(h, i // keys),
                                       start=i == 0, stop=i == kts[-1])
                    col += P
            m = T.mark(last)
            state["used", h] = (m,)
            bank.free = (finish(h, bank.ap[:, 0:2 * vw].rearrange("p (s n) -> p s n", s=2), tot, m),)

        for s in range(heads + 2):
            if s < heads:
                scores(s)
                soften(s)
            if 1 <= s <= heads:
                turn_p(s - 1)
            if s >= 2:
                values(s - 2)
        return (V.now(), A.now())


    tri = dr["tri"]
    for dst, name in ((X, "x"), (IDENT, "ident"), (DIST, "dist"), (CAUS, "causal"), (LEVEL, "levels"),
                      (RESET, "reset"), (TRIL, "tri"), (ROPE, "rope"), (CROPE, "crope"), (CMPA, "cmp_add"),
                      (CMPK, "cmp_keep"), (IOTA, "iota"), (GAINS, "gains"), (SMALL, "small"), (LBL, "b_lb_logits"),
                      (ROUT, "moe_router")):
        const_in.mark(act_e.dma_start(dst[:], dr[name]))
    consts = const_in.now()
    mem_in.mark(act_e.dma_start(XN[:], dr["mem"]))
    layer_in.mark(act_e.dma_start(FING[:], dr["final_norm"].broadcast_to([P, D])))
    ring.plan([dr["a_w_in"][c] for c in range(10)] + [dr["a_w_mem_kv"][c] for c in range(2)]
              + [dr["a_w_out"][c] for c in range(4)])
    ones = V((), vec.memset, ONES[:, :], 1.0)
    for q in (V, A, T, G):
        q.wait(consts)

    g_amix, g_amem, g_bmix, g_bmem, g_dense, g_moe = (GAINS[:, i, :] for i in range(6))

    LAM = sb("lambda", [P, 1])[:, :]
    prod = stat(2)
    z = V((), vec.memset, prod, 0.0)
    z = V((z,), vec.tensor_tensor, prod[0:64, 0:1], SMALL[0:64, 4:5], SMALL[0:64, 5:6], ALU.mult)
    z = V((), vec.tensor_tensor, prod[0:64, 1:2], SMALL[0:64, 6:7], SMALL[0:64, 7:8], ALU.mult)
    m = T((z, ones), pe_e.matmul, banks[0].ap[:, 0:2], ONES[:, :], prod, start=True, stop=True)
    e2 = stat(2)
    m = A((m,), act_e.activation, e2, banks[0].ap[:, 0:2], ACT.Exp)
    banks[0].free = (m,)
    m = V((m,), vec.tensor_tensor, LAM, e2[:, 0:1], e2[:, 1:2], ALU.subtract)
    lam_ready = V((m,), vec.tensor_scalar, LAM, LAM, LAM_INIT, None, ALU.add)
    GA = sb("gain_a", [P, KT])[:, :]
    GB = sb("gain_b", [P, KT])[:, :]
    m = V((), vec.memset, GA, 1.0)
    m = V((m,), vec.memset, GB, 1.0)
    V((m,), vec.tensor_scalar, GA[:, 0:HEADS], GA[:, 0:HEADS], SMALL[:, 0:1], 1.0 - LAM_INIT, ALU.mult, ALU.mult)
    V((m,), vec.tensor_scalar, GB[:, 0:HEADS], GB[:, 0:HEADS], SMALL[:, 1:2], None, ALU.mult)
    LB = sb("bound", [P, HEADS])[:, :]
    OMLB = sb("one_less_bound", [P, HEADS])[:, :]
    m = V((), vec.tensor_tensor, LB, LBL[:, :], LBL[:, :], ALU.subtract)
    m = A((m,), act_e.activation, LB, LB, ACT.Exp)
    m = V((m,), vec.reciprocal, OMLB, LB)
    m = V((m,), vec.tensor_tensor, OMLB, OMLB, LB, ALU.mult)
    m = V((m,), vec.tensor_tensor, LB, OMLB, OMLB, ALU.subtract)
    lb_ready = V((m,), vec.tensor_scalar, OMLB, LB, -1.0, 1.0, ALU.mult, ALU.add)

    m = tuple(A((mem_in.now(),), act_e.activation, HT[:, 4 * t:4 * t + 4, :].rearrange("p a b -> p (a b)"),
                XN[:, t, :], ACT.Square, accum_out=ST[:, 150 + t:151 + t]) for t in range(TT))
    r = root(ST[:, 150:152], TT, D, m)
    m = tuple(A((r,), act_e.activation, XN[:, t, :], XN[:, t, :], ACT.Copy, scale=ST[:, 150 + t:151 + t])
              for t in range(TT))
    memory_ready = turn(lambda t, c: XN[:, t, c * P:(c + 1) * P], KT, None, MT, m, m)
    x_ready = ()

    def mixer_memory(gain, qm, O, ready, bufs, free):
        kT, v = room(2, S), room(TT, 256)
        gm = V((*memory_ready, *free), vec.tensor_tensor, HT[:, :, :], MT[:, :, :], spread(gain, S), ALU.mult)
        mk = project(1, HT, (gm,), copy_to(kT), "columns")
        mv = project(1, HT, (gm,), copy_rows(v), "rows")

        def rows_of(h):
            return slice(64 * (h % 2), 64 * (h % 2) + 64)

        def finish(h, seen, tot, m):
            return V((m,), vec.tensor_tensor, O[:, :, 768 + h * HD:768 + (h + 1) * HD], seen, spread(tot, HD),
                     ALU.mult)

        return attend(MEM_HEADS, FULL, lambda h, m, q: qm[rows_of(h), h // 2, q * P:(q + 1) * P],
                      lambda h, m, n: kT[rows_of(h), h // 2, 0:n], lambda h, i: v[:, i, h * HD:(h + 1) * HD],
                      None, finish, (*mk, *mv, *ready), bufs, HD)

    def head_norm(O, ready):
        heads = O[:, :, 0:768]
        ssq = stat(TT * HEADS)
        for t in range(TT):
            sq = A(ready, act_e.activation, XN[:, t, 0:768], heads[:, t, :], ACT.Square)
        sq = V((sq,), vec.tensor_reduce, ssq.rearrange("p (t h) -> p t h", t=TT),
               XN[:, :, 0:768].rearrange("p t (h e) -> p t h e", h=HEADS), AX_X, ALU.add)
        r = root(ssq, 12, P, (sq,))
        for t in range(TT):
            part = heads[:, t, :].rearrange("p (h e) -> p h e", h=HEADS)
            r2 = V((r,), vec.tensor_tensor, part, part, spread(ssq[:, t * HEADS:(t + 1) * HEADS], P), ALU.mult)
        return r2


    h_ready = norm_columns(X, g_amix, HT, x_ready, memory_ready)
    used[0] = 0
    qT, kT, v, qm = room(HEADS, S), room(HEADS, S), room(TT, 768), room(2, S)
    O = room(TT, D)
    mq = project(3, HT, h_ready, copy_to(qT, HD ** -0.5), "columns")
    mk = project(3, HT, h_ready, copy_to(kT), "columns")
    mv = project(3, HT, h_ready, copy_rows(v), "rows")
    mm = project(1, HT, h_ready, copy_to(qm, HD ** -0.5), "columns")
    p_bufs = [room(2, 512), room(2, 512)], [room(512), room(512)]

    def half(m):
        return slice(64 * m, 64 * m + 64)

    def with_distance(h, mine, raw, ready):
        return V(ready, vec.scalar_tensor_tensor, mine, DIST[:, :], -SLOPES[h], raw, ALU.mult, ALU.add)

    def diff_out(h, seen, tot, m):
        return A((m,), act_e.copy, O[:, :, h * P:(h + 1) * P], seen)

    V.wait(lam_ready)
    done = attend(HEADS, TRI, lambda h, m, q: qT[half(m), h, q * P:(q + 1) * P],
                  lambda h, m, n: kT[half(m), h, 0:n], lambda h, i: v[:, i, h * P:(h + 1) * P],
                  with_distance, diff_out, (*mq, *mk, *mv), p_bufs, P, maps=2)
    normed = head_norm(O, done)
    done = mixer_memory(g_amem, qm, O, mm, p_bufs, (T.now(),))
    o_ready = turn(lambda t, c: O[:, t, c * P:(c + 1) * P], KT, GA, HT, (*done, normed), (T.now(),))
    x_ready = project(4, HT, o_ready, add_rows(X), "rows")


    def ff_tiles(n, src, width, chunk, at, base, gate_tile, fold, loop):
        ahead = before if loop else (lambda m: None)
        bank_of = [4, 5, 6, 4, 5, 6, 7]
        load_at = [s.count + 16 for s in slots]
        acts, gus, downs, reads = [None] * n, [None] * n, [None] * n, [None] * n
        T0, V0 = T.count, V.count
        order = []
        for j in range(n):
            order.append(("gu", j))
            if j:
                order.append(("down", j - 1))
        order.append(("down", n - 1))
        t_at = {o: (T, T0 + i + 1, T.turn) for i, o in enumerate(order)}

        def gate_up(j):
            w = W[:, j, 0:2 * D].rearrange("p (k n) -> p k n", k=KT)
            bank = banks[bank_of[j]]
            T.wait((slots[j], load_at[j], slots[j].turn))
            same = [i for i in range(j) if bank_of[i] == bank_of[j]]
            if same:
                T.wait(reads[same[-1]])
            elif loop:
                last_user = [i for i in range(n) if bank_of[i] == bank_of[j]][-1]
                T.wait(before((V, V0 + per_tile * (last_user + 1), V.turn)))
            for half_ in range(2):
                for i in range(KT):
                    last = pe_e.matmul(bank.ap[:, half_ * 256:half_ * 256 + width], w[:, i, half_ * P:half_ * P + P],
                                       src[:, i, 0:width], start=i == 0, stop=i == KT - 1)
            m = T.mark(last)
            assert m == t_at["gu", j]
            V.wait(*([before(t_at["down", j])] if loop else []))
            v0 = V.count
            reads[j] = gate_tile(j, bank.ap[:, 0:width], bank.ap[:, 256:256 + width], AT[:, j, 0:width], m, loop)
            assert V.count - v0 == per_tile
            bank.free = (reads[j], A.now())

        def down(j):
            wd = W[:, j, 2 * D:3 * D]
            T.wait(reads[j])
            if j == 0 and loop:
                T.wait(before((V, V0 + per_tile * n + n_fold, V.turn)))
            for t in range(width // P):
                for half_ in range(2):
                    last = pe_e.matmul(banks[2 * t + half_].ap, AT[:, j, t * P:(t + 1) * P],
                                       wd[:, half_ * 512:half_ * 512 + 512], start=j == 0, stop=j == n - 1)
            m = T.mark(last)
            assert m == t_at["down", j]

        n_fold = TT
        per_tile = gate_tile.per_tile
        if not loop:
            for b in banks:
                T.wait(*b.free)
        for kind, j in order:
            (gate_up if kind == "gu" else down)(j)
        for j in range(n):
            SP.wait(*([before(t_at["down", j])] if loop else []))
            slots[j].mark(sync.dma_start(W[:, j, 0:chunk.width], chunk(at, base + j)))
        return fold(T.now())

    class Swiglu:
        per_tile = 1

        def __call__(self, j, gate, up, dst, m, loop):
            sg = SG[:, j % 2, 0:gate.shape[-1]]
            if j >= 2:
                A.wait(self.marks[j - 2])
            elif loop:
                A.wait(before((V, self.v0 + (5 if j % 2 else 6) + 1, V.turn)))
            a = A((m,), act_e.activation, sg, gate, ACT.Silu)
            v = V((a,), vec.tensor_tensor, dst, sg, up, ALU.mult)
            self.marks[j] = v
            return v

        def start(self):
            self.marks, self.v0 = {}, V.count

    class Conv(Swiglu):
        per_tile = 7

        def __call__(self, j, gate, up, dst, m, loop):
            c = W[:, j, FFCOLS:FFCOLS + 8]
            parts = []
            for i, src in enumerate((gate, up)):
                k = c[:, 4 * i:4 * i + 4]
                buf = CV[:, i, :]
                V.wait(m)
                if i == 0:
                    V.wait(V.now())
                    if j:
                        V.wait(self.acts[j - 1])
                    elif loop:
                        V.wait(before((A, A.count + 7, A.turn)))
                v = V((), vec.tensor_scalar, buf, src, k[:, 2:3], k[:, 3:4], ALU.mult, ALU.add)
                v = V((v,), vec.scalar_tensor_tensor, buf[:, 1:S], src[:, 0:S - 1], k[:, 1:2], buf[:, 1:S],
                      ALU.mult, ALU.add)
                v = V((v,), vec.scalar_tensor_tensor, buf[:, 2:S], src[:, 0:S - 2], k[:, 0:1], buf[:, 2:S],
                      ALU.mult, ALU.add)
                parts.append(v)
            sg = SG[:, j % 2, :]
            if j >= 2:
                A.wait(self.marks[j - 2])
            elif loop:
                A.wait(before((V, self.v0 + 7 * ((5 if j % 2 else 6) + 1), V.turn)))
            a = A((parts[0],), act_e.activation, sg, CV[:, 0, :], ACT.Silu)
            self.acts[j] = a
            v = V((a, parts[1]), vec.tensor_tensor, dst, sg, CV[:, 1, :], ALU.mult)
            self.marks[j] = v
            return v

        def start(self):
            super().start()
            self.acts = {}

    def fold_rows(dst):
        def go(m):
            for t in range(TT):
                part = dst[:, t, :]
                v = V((m,), vec.tensor_tensor, part, part, PS[:, 2 * t:2 * t + 2, :].rearrange("p a b -> p (a b)"),
                      ALU.add)
            return v
        return go

    def feed_forward(chunks, turns, tail, src, kind, fold, ready):
        per = {q: 0 for q in lines}
        per.update({T: 2 * TURN, V: kind.per_tile * TURN + TT, A: TURN})
        per.update({s: 16 for s in slots})
        for b in banks:
            T.wait(*b.free)
        T.wait(*ready)
        V.wait(*ready)
        SP.wait(*[f for fr in ring.free for f in fr], T.now())
        with Turns(nc, turns, lines, per) as i:
            kind.start()
            ff_tiles(TURN, src, S, chunks, i, 0, kind, fold(i) if fold.__name__ == "by_turn" else fold, True)
        done = T.now(), V.now()
        for b in banks:
            b.free = done
        if tail:
            SP.wait(*done)
            T.wait(*done)
            A.wait(*done)
            kind.start()
            ff_tiles(tail, src, S, chunks, None, turns * TURN, kind, fold, False)
        done = T.now(), V.now(), A.now()
        for b in banks:
            b.free = done
        ring.free = [(T.now(),) for _ in slots]
        return done

    class Chunks:

        def __init__(self, ap, width=FFCOLS, first=0):
            self.ap, self.width, self.first = ap, width, first

        def __call__(self, i, j):
            at = self.first + (j if i is None else i * TURN + j)
            if isinstance(at, int):
                return self.ap[at]
            return self.ap[bass.ds(at, 1)].rearrange("o p n -> (o p) n")

    def ConvChunks(ap, layer):
        return Chunks(ap, SLOT, layer * (FF // P))

    h_ready = norm_columns(X, g_dense, HT, x_ready, x_ready)
    x_ready = feed_forward(Chunks(dr["dense_ff"]), FF // P // TURN, FF // P % TURN, HT, Swiglu(), fold_rows(X), h_ready)
    ring.plan([dr["b_w_in"][c] for c in range(13)] + [dr["b_w_mem_kv"][c] for c in range(2)]
              + [dr["b_w_out"][c] for c in range(4)])


    h_ready = norm_columns(X, g_bmix, HT, x_ready, x_ready)
    used[0] = 0
    qT, kT, F_, B_ = room(HEADS, S), room(HEADS, S), room(HEADS, S), room(HEADS, S)
    v, gate, qm = room(TT, 768), room(TT, 768), room(2, S)
    QK = room(HEADS, S)
    AIN, ACR = room(HEADS, TT, P), room(HEADS, P)
    O = XN
    mq = project(3, HT, h_ready, copy_to(qT), "columns")

    def forget(c, seen, m):
        a = A((m,), act_e.activation, F_[:, 2 * c:2 * c + 2, :], seen, ACT.Sigmoid)
        b = A((m,), act_e.activation, kT[:, 2 * c:2 * c + 2, :], seen, ACT.Sigmoid, scale=-1.0)
        return (b,)

    mf = project(3, HT, h_ready, forget, "columns")
    mv = project(3, HT, h_ready, copy_rows(v), "rows")
    mg = project(3, HT, h_ready, copy_rows(gate, func=ACT.Silu), "rows")
    mm = project(1, HT, h_ready, copy_to(qm, HD ** -0.5), "columns")
    V.wait(lb_ready, *mf)
    for h in range(HEADS):
        V((), vec.tensor_scalar, F_[:, h, :], F_[:, h, :], OMLB[:, h:h + 1], LB[:, h:h + 1], ALU.mult, ALU.add)
        V((), vec.tensor_scalar, kT[:, h, :], kT[:, h, :], OMLB[:, h:h + 1], None, ALU.mult)
    k_ready = V.now()
    m = V((k_ready,), vec.tensor_scalar, F_[:, :, :], F_[:, :, :], 2.0 ** -63, None, ALU.max)
    m = A((m,), act_e.activation, F_[:, :, :], F_[:, :, :], ACT.Ln)
    for h in range(HEADS):
        m2 = V((m,), vec.tensor_tensor_scan, B_[:, h, :], RESET[:, :], F_[:, h, :], 0.0, ALU.mult, ALU.add)
    b_ready = m2
    zero = V((), vec.memset, AIN[:, :, :, :], 0.0)

    def level_matmuls(lhs, rhs, ready, mask):
        for h0 in range(0, HEADS, 2):
            bank = next_bank()
            T.wait(ready, *bank.free)
            for h in (h0, h0 + 1):
                for t in range(TT):
                    c = ((h - h0) * TT + t) * P
                    cut = slice(t * P, (t + 1) * P)
                    last = pe_e.matmul(bank.ap[:, c:c + P], lhs[:, h, cut], rhs[:, h, cut], start=True, stop=True)
            m = T.mark(last)
            into = AIN[:, h0:h0 + 2, :, :].rearrange("p h t n -> p (h t) n")
            seen = bank.ap.rearrange("p (a n) -> p a n", n=P)
            m = V((m, zero), vec.copy_predicated, into, mask.unsqueeze(1).broadcast_to([P, 4, P]), seen)
            bank.free = (m,)
        return m

    level_matmuls(kT, qT, k_ready, LEVEL[:, 7, :])
    exps_read = b_ready
    prods = ()
    for lv in range(7):
        n = 1 << lv
        def cut(ap):
            return ap.rearrange("p h (b s n) -> p (h b) s n", s=2, n=n)
        E, B4, Q4 = cut(F_), cut(B_), cut(QK)
        mid = B4[:, :, 0, n - 1:n]
        nb = B4.shape[1]
        V.wait(b_ready, *([exps_read]))
        V((), vec.tensor_tensor, E[:, :, 0, :], mid.broadcast_to([P, nb, n]), B4[:, :, 0, :], ALU.subtract)
        if n < CH:
            m = V((), vec.tensor_tensor, E[:, :, 1, :], B4[:, :, 1, :], mid.broadcast_to([P, nb, n]), ALU.subtract)
        else:
            m = V((), vec.tensor_copy, E[:, :, 1, :], B4[:, :, 1, :])
        m = A((m,), act_e.activation, F_[:, :, :], F_[:, :, :], ACT.Exp)
        V.wait(m, T.now())
        V((), vec.tensor_tensor, Q4[:, :, 0, :], E[:, :, 0, :], cut(kT)[:, :, 0, :], ALU.mult)
        m = exps_read = V((), vec.tensor_tensor, Q4[:, :, 1, :], E[:, :, 1, :], cut(qT)[:, :, 1, :], ALU.mult)
        level_matmuls(QK, QK, m, LEVEL[:, lv, :])
    ends = [B_[:, :, (c + 1) * CH - 1:(c + 1) * CH] for c in range(4)]
    def chunk(ap, c):
        return ap[:, :, c * CH:(c + 1) * CH]
    def wide(ap):
        return ap.broadcast_to([P, HEADS, CH])
    V.wait(exps_read)
    m = V((), vec.tensor_tensor, chunk(F_, 0), wide(ends[0]), chunk(B_, 0), ALU.subtract)
    V((m,), vec.tensor_tensor, chunk(F_, 0), chunk(F_, 0), wide(ends[1]), ALU.add)
    V((), vec.tensor_tensor, chunk(F_, 1), wide(ends[1]), chunk(B_, 1), ALU.subtract)
    V((), vec.tensor_copy, chunk(F_, 2), chunk(B_, 2))
    m = V((), vec.tensor_tensor, chunk(F_, 3), chunk(B_, 3), wide(ends[2]), ALU.add)
    m = A((m,), act_e.activation, F_[:, :, :], F_[:, :, :], ACT.Exp)
    V.wait(m, T.now())
    V((), vec.tensor_tensor, QK[:, :, 0:P], F_[:, :, 0:P], kT[:, :, 0:P], ALU.mult)
    m = V((), vec.tensor_tensor, QK[:, :, P:S], F_[:, :, P:S], qT[:, :, P:S], ALU.mult)
    for h0 in (0, 4):
        bank = next_bank()
        T.wait(m, *bank.free)
        w = min(4, HEADS - h0)
        for h in range(h0, h0 + w):
            last = pe_e.matmul(bank.ap[:, (h - h0) * P:(h - h0 + 1) * P], QK[:, h, 0:P], QK[:, h, P:S], start=True,
                               stop=True)
        mc = T.mark(last)
        bank.free = (A((mc,), act_e.copy, ACR[:, h0:h0 + w, :],
                       bank.ap[:, 0:w * P].rearrange("p (h n) -> p h n", h=w)),)
    a_ready = (V.now(), A.now())
    for t in range(TT):
        for h0 in (0, 4):
            bank = next_bank()
            w = min(4, HEADS - h0)
            T.wait(*a_ready, *mv, *bank.free)
            for h in range(h0, h0 + w):
                to = bank.ap[:, (h - h0) * P:(h - h0 + 1) * P]
                last = pe_e.matmul(to, AIN[:, h, t, :], v[:, t, h * P:(h + 1) * P], start=True, stop=t == 0)
                if t:
                    last = pe_e.matmul(to, ACR[:, h, :], v[:, 0, h * P:(h + 1) * P], start=False, stop=True)
            mo = T.mark(last)
            bank.free = (A((mo,), act_e.copy, O[:, t, h0 * P:(h0 + w) * P], bank.ap[:, 0:w * P]),)
    heads = O[:, :, 0:768]
    ssq = stat(TT * HEADS)
    SQ = QK.rearrange("p h n -> p (h n)").rearrange("p (t n) -> p t n", t=TT)
    m = A((A.now(), T.now()), act_e.activation, SQ, heads, ACT.Square)
    m = V((m,), vec.tensor_reduce, ssq.rearrange("p (t h) -> p t h", t=TT),
          SQ.rearrange("p t (h e) -> p t h e", h=HEADS), AX_X, ALU.add)
    r = root(ssq, 12, P, (m,))
    for t in range(TT):
        part = heads[:, t, :].rearrange("p (h e) -> p h e", h=HEADS)
        m = V((r,), vec.tensor_tensor, part, part, spread(ssq[:, t * HEADS:(t + 1) * HEADS], P), ALU.mult)
    gated = V((m, *mg), vec.tensor_tensor, heads, heads, gate[:, :, :], ALU.mult)
    used[0] = 2 * HEADS * S
    p_bufs = [QK.rearrange("p h n -> p (h n)")[:, 0:512].unsqueeze(1), QK.rearrange("p h n -> p (h n)")[:, 512:1024].unsqueeze(1)], \
        [AIN.rearrange("p h t n -> p (h t n)")[:, 0:512], AIN.rearrange("p h t n -> p (h t n)")[:, 512:1024]]
    for q in (V, A, T):
        q.wait(gated, T.now(), A.now())
    done = mixer_memory(g_bmem, qm, O, mm, p_bufs, (T.now(), gated))
    o_ready = turn(lambda t, c: O[:, t, c * P:(c + 1) * P], KT, GB, HT, (*done, gated), (T.now(),))
    x_ready = project(4, HT, o_ready, add_rows(X), "rows")


    h_ready = norm_columns(X, g_moe, HT, x_ready, x_ready)
    COMB = sb("expert_weight", [P, TT, NE, FE // P // TURN])
    lg, top8, hot = stat(TT * NE), stat(8), stat(NE)
    hot2 = stat(NE)
    idxf = stat(2)
    w12 = stat(4)
    for t in range(TT):
        bank = banks[t]
        T.wait(*h_ready, *bank.free)
        for i in range(KT):
            last = pe_e.matmul(bank.ap[:, 0:NE], HT[:, i, t * P:(t + 1) * P], ROUT[:, i, :], start=i == 0,
                               stop=i == KT - 1)
        m = T.mark(last)
        mine = lg[:, t * NE:(t + 1) * NE]
        m = V((m,), vec.tensor_copy, mine, bank.ap[:, 0:NE])
        bank.free = (m,)
        m = V((m,), vec.max, top8, mine)
        m = V((m,), vec.max_index, STI[:, 0:8], top8, mine)
        m = V((m,), vec.tensor_copy, idxf, STI[:, 0:2])
        m = V((m,), vec.tensor_tensor, w12[:, 0:1], top8[:, 1:2], top8[:, 0:1], ALU.subtract)
        e = A((m,), act_e.activation, w12[:, 1:2], w12[:, 0:1], ACT.Exp)
        m = V((e,), vec.tensor_scalar, w12[:, 2:3], w12[:, 1:2], 1.0, None, ALU.add)
        m = V((m,), vec.reciprocal, w12[:, 2:3], w12[:, 2:3])
        m = V((m,), vec.tensor_tensor, w12[:, 3:4], w12[:, 1:2], w12[:, 2:3], ALU.mult)
        m = V((m,), vec.tensor_scalar, hot, IOTA[:, :], idxf[:, 0:1], w12[:, 2:3], ALU.is_equal, ALU.mult)
        m = V((m,), vec.tensor_scalar, hot2, IOTA[:, :], idxf[:, 1:2], w12[:, 3:4], ALU.is_equal, ALU.mult)
        m = V((m,), vec.tensor_tensor, hot, hot, hot2, ALU.add)
        m = V((m,), vec.tensor_copy, COMB[:, t, :, :], spread(hot, FE // P // TURN))

    def by_turn(i):
        def go(m):
            for t in range(TT):
                part = X[:, t, :]
                w = COMB[:, t, :, :].rearrange("p e r -> p (e r)")[:, bass.ds(i, 1)]
                v = V((m,), vec.scalar_tensor_tensor, part, PS[:, 2 * t:2 * t + 2, :].rearrange("p a b -> p (a b)"),
                      w, part, ALU.mult, ALU.add)
            return v
        return go

    x_ready = feed_forward(Chunks(dr["moe_ff"]), NE * FE // P // TURN, 0, HT, Swiglu(), by_turn, (*h_ready, m))

    m = rms_scale(X, XN, D, x_ready, (T.now(), V.now()))
    for t in range(TT):
        m2 = V((*m, layer_in.now()), vec.tensor_tensor, X[:, t, :], XN[:, t, :], FING[:, :], ALU.mult)

    NL = 2
    PL = sb("layer_columns", [P, 536])
    B2 = sb("compressed_bias", [NC, 2, HD])
    with nc.Fori(0, NL) as layer:
        nc.all_engine_barrier()
        for q in lines:
            pool_e.sem_clear(q.sem)
            q.reset()
        nc.all_engine_barrier()
        ring.reset()
        for b in banks:
            b.free = ()

        def of_layer(name, c=0, n=1):
            return dr[name][bass.ds(layer * n + c, 1)].rearrange("o p n -> (o p) n")

        used[0] = 0
        ZQK, ZV, ZC = room(TT, 768), room(TT, 256), room(TT, 256)
        spare = used[0]
        ZD, ZT = room(TT, 512), room(4, S)
        FL, HC = room(2, GROUPS * NC, PAIRS), room(2, 2, GROUPS * NC)
        KVC, KCT, QKT = room(4 * HD)[0:NC], room(NC), room(6, S)
        MX, VV, WS, LN, RG = room(TT, D), room(TT, 512), room(8, P), room(2, 512), room(D)
        GT = room(TT, GW)
        CV = ARENA[:, 0:512].rearrange("p (a b) -> p a b", a=2)
        PLT = ARENA[:, 512:1024].rearrange("p (a b) -> p a b", a=2)
        buf = [ARENA[:, spare + 512 * i:spare + 512 * (i + 1)] for i in range(4)]
        p_bufs = [buf[0].unsqueeze(1), buf[1].unsqueeze(1)], [buf[2], buf[3]]

        for dst, src in ((PL[:, :], of_layer("layer_columns")),
                         (B2[:, :, :].rearrange("p a b -> p (a b)"), of_layer("cmp_b2").broadcast_to([NC, 2 * HD])),
                         (WS.rearrange("p a b -> p (a b)"), of_layer("gmlp_ws")),
                         (LN.rearrange("p a b -> p (a b)"), of_layer("gmlp_ln").broadcast_to([P, D])),
                         (FING[:, :], of_layer("post_mix_g").broadcast_to([P, D])),
                         (RG, of_layer("post_ffn_g").broadcast_to([P, D]))):
            layer_in.mark(act_e.dma_start(dst, src))
        params = layer_in.now()
        ring.plan([of_layer("w_in", c, 9) for c in range(9)] + [of_layer("cmp_w1", c, 4) for c in range(4)]
                  + [of_layer("w_o", c, 4) for c in range(4)])
        for q in (V, A, T):
            q.wait(params)
        g_pre, g_ffn, g_ple, g_mix = (PL[:, 8 * i:8 * i + 8] for i in range(4))
        b1 = PL[:, 32:36]
        bs = PL[:, 36:44]
        wg = PL[:, 44:236].rearrange("p (k n) -> p k n", k=KT)
        pe_col = PL[:, 236:268].rearrange("p (k n) -> p k n", k=2)
        w2 = PL[:, 268:524].rearrange("p (k h n) -> p k h n", k=2, h=2)

        h_ready = norm_columns(X, g_pre, HT, ())

        def evac_qk(c, seen, m):
            return (A((m,), act_e.activation, ZQK[:, :, c * 256:(c + 1) * 256], seen, ACT.Copy,
                      scale=HD ** -0.5 if c < 2 else 1.0),)

        mqk = project(3, HT, h_ready, evac_qk, "rows")
        mv = project(1, HT, h_ready, copy_rows(ZV), "rows")
        mc = project(1, HT, h_ready, copy_rows(ZC), "rows")

        def rope(z, cs, heads, ready):
            n = z.shape[0]
            x1, x2 = z[:, :, 0:8], z[:, :, 8:16]
            cos = cs[:, 0:8].unsqueeze(1).broadcast_to([n, heads, 8])
            sin = cs[:, 8:16].unsqueeze(1).broadcast_to([n, heads, 8])
            tmp = RT[0:n].rearrange("p (k h n) -> p k h n", k=4, h=12)[:, :, 0:heads, :]
            V.wait(V.now())
            V(ready, vec.tensor_tensor, tmp[:, 0], x1, cos, ALU.mult)
            V((), vec.tensor_tensor, tmp[:, 1], x2, sin, ALU.mult)
            V((), vec.tensor_tensor, tmp[:, 2], x2, cos, ALU.mult)
            m = V((), vec.tensor_tensor, tmp[:, 3], x1, sin, ALU.mult)
            V((m,), vec.tensor_tensor, x1, tmp[:, 0], tmp[:, 1], ALU.subtract)
            return V((), vec.tensor_tensor, x2, tmp[:, 2], tmp[:, 3], ALU.add)

        RT = VV[:, 0, 0:384]
        for t in range(TT):
            rm = rope(ZQK[:, t, :].rearrange("p (h d) -> p h d", h=12), ROPE[:, t, :], 12, mqk)
        qk_ready = turn(lambda t, c: ZQK[:, t, c * P:(c + 1) * P], 6, None, QKT, (rm,))
        for t in range(TT):
            dup = A(mc, act_e.copy, ZD[:, t, :].rearrange("p (g u d) -> p g u d", g=4, u=2),
                    ZC[:, t, :].rearrange("p (g d) -> p g d", g=4).unsqueeze(2).broadcast_to([P, 4, 2, HD]))
        c_ready = turn(lambda t, c: ZD[:, t, c * P:(c + 1) * P], 4, None, ZT, (dup,))
        V.wait(*c_ready)
        Z16 = ZT.rearrange("p g (n l) -> p g n l", l=CSTR)
        F16 = FL.rearrange("p k (g n) j -> p k g n j", g=GROUPS)
        for kv in range(2):
            for odd in range(2):
                for late in range(2):
                    rows_ = half(odd)
                    V((), vec.tensor_tensor, F16[rows_, kv, :, :, 8 * late:8 * late + 8],
                      Z16[rows_, 2 * kv:2 * kv + 2, late:late + NC, odd:CSTR:2],
                      pe_col[rows_, kv, 8 * late:8 * late + 8].unsqueeze(1).unsqueeze(1)
                      .broadcast_to([64, GROUPS, NC, 8]), ALU.add)
        blocks_ready = V.now()

        bank = next_bank()
        T.wait(*h_ready, *bank.free)
        for t in range(TT):
            for i in range(KT):
                last = pe_e.matmul(bank.ap[:, t * GW:(t + 1) * GW], HT[:, i, t * P:(t + 1) * P], wg[:, i, :],
                                   start=i == 0, stop=i == KT - 1)
        m = T.mark(last)
        gates = A((m,), act_e.activation, GT, bank.ap[:, 0:TT * GW].rearrange("p (t n) -> p t n", t=TT), ACT.Sigmoid)
        bank.free = (gates,)
        mu = project(2, HT, h_ready, copy_rows(MX[:, :, 512:D], func=ACT.Gelu_apprx_tanh), "rows")
        A.wait(rm)
        mvv = project(2, HT, h_ready, copy_rows(VV, func=ACT.Gelu_apprx_tanh), "rows")

        for kv in range(2):
            pair = banks[2 * kv], banks[2 * kv + 1]
            T.wait(blocks_ready, *pair[0].free, *pair[1].free)
            for part in range(2):
                k, w, arrived = ring.take()
                w = w[:, 0:8 * 256].rearrange("p (k n) -> p k n", k=8)
                T.wait(arrived)
                for hid in range(2):
                    for j in range(8):
                        last = pe_e.matmul(pair[hid].ap[:, 0:GROUPS * NC], w[:, j, hid * P:(hid + 1) * P],
                                           FL[:, kv, :, 8 * part + j], start=part == 0 and j == 0,
                                           stop=part == 1 and j == 7)
                m = T.mark(last)
                ring.give(k, m)
            for hid in range(2):
                a = A((m,), act_e.activation, HC[:, kv, hid, :], pair[hid].ap[:, 0:GROUPS * NC],
                      ACT.Gelu_apprx_tanh, bias=b1[:, 2 * kv + hid:2 * kv + hid + 1])
                pair[hid].free = (a,)
        bank = next_bank()
        T.wait(a, *bank.free)
        for kv in range(2):
            for g in range(GROUPS):
                c = (kv * GROUPS + g) * HD
                for hid in range(2):
                    last = pe_e.matmul(bank.ap[0:NC, c:c + HD], HC[:, kv, hid, g * NC:(g + 1) * NC],
                                       w2[:, kv, hid, :], start=hid == 0, stop=hid == 1)
        m = T.mark(last)
        kvc = KVC.rearrange("p (k g d) -> p k g d", k=2, g=GROUPS)
        m = V((m,), vec.tensor_tensor, kvc, bank.ap[0:NC, 0:256].rearrange("p (k g d) -> p k g d", k=2, g=GROUPS),
              B2[:, :, :].unsqueeze(2).broadcast_to([NC, 2, GROUPS, HD]), ALU.add)
        bank.free = (m,)
        RT = XN[:, 0, 0:384]
        m = rope(kvc[:, 0], CROPE[:, :], GROUPS, (m,))
        bank = next_bank()
        T.wait(*bank.free)
        m = T((m,), pe_e.transpose, bank.ap[:, 0:NC], KVC[:, 0:GROUPS * HD], IDENT[0:NC, 0:NC])
        kct_ready = V((m,), vec.tensor_copy, KCT, bank.ap[:, 0:NC])
        bank.free = (kct_ready,)

        def add_mask(mask):
            def go(h, mine, raw, ready):
                return V(ready, vec.tensor_tensor, mine, raw, mask, ALU.add)
            return go

        V.wait(gates)

        def branch(br):
            def finish(h, seen, tot, m):
                o = MX[:, :, h * HD:(h + 1) * HD]
                w = stat(TT)
                g = V((m,), vec.tensor_tensor, w, tot, GT[:, :, 3 * h + br], ALU.mult)
                if br == 0:
                    return V((g,), vec.tensor_tensor, o, seen, spread(w, HD), ALU.mult)
                for t in range(TT):
                    g = V((g,), vec.scalar_tensor_tensor, o[:, t, :], seen[:, t, :], w[:, t:t + 1], o[:, t, :],
                          ALU.mult, ALU.add)
                return g
            return finish

        def query(h, m, q):
            return QKT[half(h // 4), h % 4, q * P:(q + 1) * P]

        cmp_segs = [(0, NC, 0), (1, NC, NC)]
        attend(NH2, cmp_segs, query, lambda h, m, n: KCT[half(h // 4), :],
               lambda h, i: KVC[:, (GROUPS + h // 4) * HD:(GROUPS + h // 4 + 1) * HD],
               add_mask(CMPA[:, :, :].rearrange("p t n -> p (t n)")), branch(0), (*qk_ready, kct_ready), p_bufs, HD,
               keys=NC, keep=CMPK[:, :, :].rearrange("p t n -> p (t n)"))
        for br in (1, 2):
            def value(h, i, br=br):
                c = ((br - 1) * GROUPS + h // 4) * HD
                return ZV[:, i, c:c + HD]
            done = attend(NH2, TRI, query, lambda h, m, n, br=br: QKT[half(h // 4), 3 + br, 0:n], value,
                          add_mask(CAUS[:, :]), branch(br), (*qk_ready, *mv, V.now(), A.now()), p_bufs, HD)

        wsm = V((), vec.tensor_tensor, WS, WS, TRIL[:, :].unsqueeze(1).broadcast_to([P, 8, P]), ALU.mult)
        V.wait(*mvv)
        bn, mv2 = stat(12), stat(4)
        for t in range(TT):
            m = V((), vec.bn_stats, bn[:, 6 * t:6 * t + 6], VV[:, t, :])
            m = V((m,), vec.bn_aggr, mv2[:, 2 * t:2 * t + 2], bn[:, 6 * t:6 * t + 6])
            m = V((m,), vec.tensor_scalar, mv2[:, 2 * t + 1:2 * t + 2], mv2[:, 2 * t + 1:2 * t + 2], EPS, None, ALU.add)
            m = A((m,), act_e.activation, mv2[:, 2 * t + 1:2 * t + 2], mv2[:, 2 * t + 1:2 * t + 2], ACT.Sqrt)
            m = V((m,), vec.reciprocal, mv2[:, 2 * t + 1:2 * t + 2], mv2[:, 2 * t + 1:2 * t + 2])
            m = V((m,), vec.tensor_scalar, VV[:, t, :], VV[:, t, :], mv2[:, 2 * t:2 * t + 1],
                  mv2[:, 2 * t + 1:2 * t + 2], ALU.subtract, ALU.mult)
            m = V((m,), vec.tensor_tensor, VV[:, t, :], VV[:, t, :], LN[:, 0, :], ALU.mult)
            ln = V((m,), vec.tensor_tensor, VV[:, t, :], VV[:, t, :], LN[:, 1, :], ALU.add)
        V.wait(*mu)
        for t in range(TT):
            bank = next_bank()
            T.wait(ln, *bank.free)
            for g in range(8):
                last = pe_e.matmul(bank.ap[:, g * HD:(g + 1) * HD], WS[:, g, :], VV[:, t, g * HD:(g + 1) * HD],
                                   start=True, stop=True)
            m = T.mark(last)
            m = V((m,), vec.tensor_tensor, VV[:, t, :].rearrange("p (g d) -> p g d", g=8),
                  bank.ap.rearrange("p (g d) -> p g d", g=8), spread(bs, HD), ALU.add)
            bank.free = (m,)
            mlp = V((m,), vec.tensor_tensor, MX[:, t, 512:D], MX[:, t, 512:D], VV[:, t, :], ALU.mult)

        ssq = stat(4)
        A.wait(*done, mlp, T.now())
        for t in range(TT):
            for s in range(2):
                m = A((), act_e.activation, XN[:, t, s * 512:(s + 1) * 512], MX[:, t, s * 512:(s + 1) * 512],
                      ACT.Square, accum_out=ssq[:, 2 * t + s:2 * t + s + 1])
        r = root(ssq, 4, 512, (m,))
        for t in range(TT):
            for s in range(2):
                m = A((r,), act_e.activation, MX[:, t, s * 512:(s + 1) * 512], MX[:, t, s * 512:(s + 1) * 512],
                      ACT.Copy, scale=ssq[:, 2 * t + s:2 * t + s + 1])
        mix_ready = turn(lambda t, c: MX[:, t, c * P:(c + 1) * P], KT, g_mix, HT, (m,), (T.now(),))
        made = project(4, HT, mix_ready, copy_rows(XN), "rows")

        def add_normed(gain, ready):
            m = rms_scale(XN, MX, D, ready, (T.now(), V.now()))
            for t in range(TT):
                v = V((m[t],), vec.tensor_tensor, MX[:, t, :], MX[:, t, :], gain, ALU.mult)
                v = V((v,), vec.tensor_tensor, X[:, t, :], X[:, t, :], MX[:, t, :], ALU.add)
            return v

        x_ready = add_normed(FING[:, :], made)

        h_ready = norm_columns(X, g_ffn, HT, (x_ready,), (x_ready,))
        zero = V((*h_ready, T.now()), vec.memset, XN[:, :, :], 0.0)
        done = feed_forward(ConvChunks(dr["conv_ff"], layer), FF // P // TURN, FF // P % TURN, HT, Conv(),
                            fold_rows(XN), (*h_ready, zero))
        ring.plan([of_layer("w_ple_proj")] + [of_layer("w_ple_gate", c, 4) for c in range(4)])
        p_in = layer_in.mark(act_e.dma_start(PLT.rearrange("p a b -> p (a b)"), of_layer("p_columns")))
        x_ready = add_normed(RG, done)

        h_ready = norm_columns(X, g_ple, HT, (x_ready,), (x_ready,))
        k, w, arrived = ring.take()
        w = w[:, 0:2 * D].rearrange("p (k n) -> p k n", k=2)
        T.wait(arrived, layer_in.now())
        for b in banks[0:4]:
            T.wait(*b.free)
        for t in range(TT):
            for s in range(2):
                for i in range(2):
                    last = pe_e.matmul(banks[2 * t + s].ap, PLT[:, i, t * P:(t + 1) * P],
                                       w[:, i, s * 512:(s + 1) * 512], start=i == 0, stop=i == 1)
        ple = T.mark(last)
        ring.give(k, ple)
        gm = project(4, HT, h_ready, copy_rows(MX, func=ACT.Sigmoid), "rows")
        for t in range(TT):
            v = V((*gm, ple), vec.tensor_tensor, MX[:, t, :], MX[:, t, :],
                  PS[:, 2 * t:2 * t + 2, :].rearrange("p a b -> p (a b)"), ALU.mult)
            v = V((v,), vec.tensor_tensor, X[:, t, :], X[:, t, :], MX[:, t, :], ALU.add)

    stored.mark(sync_wait_store(SP, (V.now(),), sync, out, X))
    sync.wait_ge(stored.sem, stored.count)


def sync_wait_store(SP, ready, sync, out, X):
    SP.wait(*ready)
    return sync.dma_start(out, X[:])


def constants():
    f = np.float32
    c = {"ident": np.eye(P, dtype=f)}
    q, k = np.arange(S)[:, None], np.arange(S)[None, :]

    def tri(a):
        return np.concatenate([a[0:P, 0:P], a[P:S, :]], axis=1).astype(f)

    c["dist"] = tri(np.where(k // CH <= q // CH, np.abs(q - k), FAR))
    c["causal"] = tri(np.where(k <= q, 0.0, NEG))
    s, t = np.arange(P)[:, None], np.arange(P)[None, :]
    levels = [((s // (2 * n) == t // (2 * n)) & (s // n % 2 == 0) & (t // n % 2 == 1)) for n in (1 << lv for lv in range(7))]
    c["levels"] = np.stack(levels + [s == t], axis=1).astype(np.int32)
    c["reset"] = np.broadcast_to((np.arange(S) % CH != 0).astype(f), (P, S)).copy()
    c["tri"] = (s <= t).astype(f)
    inv = f(500000.0) ** (-np.arange(8, dtype=f) / f(8))

    def rope(pos):
        ang = pos.astype(f)[:, None] * inv[None, :]
        return np.concatenate([np.cos(ang), np.sin(ang)], axis=1).astype(f)

    c["rope"] = rope(np.arange(S)).reshape(TT, P, 16).transpose(1, 0, 2).copy()
    c["crope"] = rope(np.arange(NC) * CSTR + 31)
    ok = (np.arange(NC) * CSTR + 31)[None, :] <= np.arange(S)[:, None]
    c["cmp_add"] = np.where(ok, 0.0, NEG).astype(f).reshape(TT, P, NC).transpose(1, 0, 2).copy()
    c["cmp_keep"] = ok.astype(f).reshape(TT, P, NC).transpose(1, 0, 2).copy()
    c["iota"] = np.broadcast_to(np.arange(NE, dtype=f), (P, NE)).copy()
    return c


def chunked(w, n=256):
    K, N = w.shape
    return w.reshape(K // P, P, N // n, n).transpose(2, 1, 0, 3).reshape(N // n, P, K // P * n)


def columns(g):
    return g.reshape(-1, P).T


def rows(a):
    return a.reshape(TT, P, -1).transpose(1, 0, 2)


def ff_chunks(gate_up, down, extra=None):
    F = down.shape[0]
    gu = gate_up.reshape(KT, P, 2, F // P, P).transpose(3, 1, 0, 2, 4).reshape(F // P, P, 2 * D)
    parts = [gu, down.reshape(F // P, P, D)]
    if extra is not None:
        parts.append(extra)
    return np.concatenate(parts, axis=2)


def lay_out(a):
    L = {"x": rows(a["x"][0]), "mem": rows(a["mem"][0])}
    L["a_w_in"] = chunked(a["a_w_in"][0])
    L["a_w_mem_kv"] = chunked(a["a_w_mem_kv"][0])
    L["a_w_out"] = chunked(a["a_w_out"][0])
    L["b_w_in"] = chunked(a["b_w_in"][0])
    L["b_w_mem_kv"] = chunked(a["b_w_mem_kv"][0])
    L["b_w_out"] = chunked(a["b_w_out"][0])
    L["dense_ff"] = ff_chunks(a["dense_w_gate_up"][0], a["dense_w_down"][0])
    L["moe_ff"] = np.concatenate([ff_chunks(a["moe_w_gate_up"][0, e], a["moe_w_down"][0, e]) for e in range(NE)])
    L["gains"] = np.stack([columns(g) for g in (a["a_norm_mix"][0], a["a_mem_norm"][0], a["b_norm_mix"][0],
                                                a["b_mem_norm"][0], a["dense_norm"][0], a["moe_norm"][0],
                                                a["final_norm"])], axis=1)
    small = np.zeros((P, 10), np.float32)
    small[:, 0] = a["a_subln"][0]
    small[:, 1] = a["b_out_norm"][0]
    for i, n in enumerate(("a_lam_q1", "a_lam_k1", "a_lam_q2", "a_lam_k2")):
        small[0:HD, 4 + i] = a[n][0]
    L["small"] = small
    L["b_lb_logits"] = columns(a["b_lb_logits"][0])
    L["moe_router"] = a["moe_router"][0].reshape(KT, P, NE).transpose(1, 0, 2)
    L["final_norm"] = a["final_norm"].reshape(1, D)
    NLAY = a["w_in_2"].shape[0]
    w = a["w_in_2"]
    order = [0, 4, 1, 5, 2, 6, 3, 7]
    q, kc, vc, ks, vs, kw, vw, g, u, v = np.split(w, np.cumsum([512] + [P] * 6 + [GW, 512]), axis=2)
    q = np.concatenate([q[:, :, h * HD:(h + 1) * HD] for h in order], axis=2)
    w = np.concatenate([q, ks, kw, vs, vw, kc, vc, u, v], axis=2)
    L["w_in"] = np.concatenate([chunked(w[i]) for i in range(NLAY)])
    L["cmp_w1"] = np.concatenate([chunked(a["cmp_w1_2"][i, k, h * D:(h + 1) * D]) for i in range(NLAY)
                                  for k in range(2) for h in range(2)])
    L["w_o"] = np.concatenate([chunked(a["w_o_2"][i]) for i in range(NLAY)])
    L["w_ple_gate"] = np.concatenate([chunked(a["w_ple_gate_2"][i]) for i in range(NLAY)])
    L["w_ple_proj"] = a["w_ple_proj_2"].reshape(NLAY, 2, P, D).transpose(0, 2, 1, 3).reshape(NLAY, P, 2 * D)
    L["p_columns"] = a["p_2"][:, 0].reshape(NLAY, S, 2, P).transpose(0, 3, 2, 1).reshape(NLAY, P, 2 * S)
    L["gmlp_ws"] = a["gmlp_ws_2"].transpose(0, 3, 1, 2).reshape(NLAY, P, 8 * P)
    L["gmlp_ln"] = np.concatenate([a["gmlp_ln_g_2"], a["gmlp_ln_b_2"]], axis=1).reshape(NLAY, 1, D)
    L["post_mix_g"] = a["post_mix_g_2"].reshape(NLAY, 1, D)
    L["post_ffn_g"] = a["post_ffn_g_2"].reshape(NLAY, 1, D)
    L["cmp_b2"] = a["cmp_b2_2"].reshape(NLAY, 1, 2 * HD)
    cols = np.zeros((NLAY, P, 536), np.float32)
    for i in range(NLAY):
        cols[i, :, 0:8] = columns(a["pre_mix_g_2"][i])
        cols[i, :, 8:16] = columns(a["pre_ffn_g_2"][i])
        cols[i, :, 16:24] = columns(a["ple_norm_g_2"][i])
        cols[i, :, 24:28] = columns(a["attn_out_g_2"][i])
        cols[i, :, 28:32] = columns(a["mlp_out_g_2"][i])
        cols[i, :, 32:36] = columns(a["cmp_b1_2"][i].reshape(-1))
        cols[i, :, 36:44] = a["gmlp_bs_2"][i].T
        cols[i, :, 44:236] = g[i].reshape(KT, P, GW).transpose(1, 0, 2).reshape(P, KT * GW)
        cols[i, :, 236:268] = a["cmp_pe_2"][i].reshape(2, PAIRS, P).transpose(2, 0, 1).reshape(P, 2 * PAIRS)
        cols[i, :, 268:524] = a["cmp_w2_2"][i].reshape(2, 2, P, HD).transpose(2, 0, 1, 3).reshape(P, 4 * HD)
    L["layer_columns"] = cols
    conv = np.concatenate([a["conv_w_2"], a["conv_b_2"][:, None]], axis=1)
    conv = conv.reshape(NLAY, 4, 2, FF // P, P).transpose(0, 3, 4, 2, 1).reshape(NLAY, FF // P, P, 8)
    L["conv_ff"] = np.concatenate([ff_chunks(a["w_up_2"][i], a["w_down_2"][i], conv[i]) for i in range(NLAY)])
    return L


def kernel(**inputs):
    import concourse.bacc as _bacc
    from concourse.bass_utils import run_bass_kernel_spmd as _run

    nc = _bacc.Bacc("TRN2", target_bir_lowering=False, num_devices=1)
    arrays, dr = {}, {}
    for name, a in {**lay_out({k: np.asarray(v) for k, v in inputs.items()}), **constants()}.items():
        a = np.ascontiguousarray(a)
        arrays[f"in_{name}"] = a
        dr[name] = nc.dram_tensor(f"in_{name}", a.shape, mybir.dt.from_np(a.dtype), kind="ExternalInput").ap()
    out = nc.dram_tensor("out_rows", (P, TT, D), F32, kind="ExternalOutput").ap()
    program(nc, dr, out)
    r = _run(nc, [arrays], core_ids=[0])
    return r.results[0]["out_rows"].transpose(1, 0, 2).reshape(1, S, D)
```

```python
import numpy as np
import concourse.bass as bass
from concourse import mybir
from concourse.alu_op_type import AluOpType as ALU

F32 = mybir.dt.float32
F32R = mybir.dt.float32r
I32 = mybir.dt.int32
U8 = mybir.dt.uint8
U32 = mybir.dt.uint32
ACT = mybir.ActivationFunctionType
AX_X = mybir.AxisListType.X

P = 128
S = 256
TT = S // P
D = 1024
KT = D // P
EPS = 1e-6
NEG = -1e30
FAR = 1e32

HEADS = 6
MEM_HEADS = 4
HD = 64
CH = 64
LAM_INIT = 0.8 - 0.6 * float(np.exp(-0.3 * 0))
SLOPES = [float(np.float32(2.0 ** (-8.0 * (h + 1) / HEADS))) for h in range(HEADS)]

FF = 2816
FE = 3584
NE = 8
TURN = 4
POOL_SHARE = 768
CAP = P

NH2 = 8
GROUPS = 2
NC = 15
CSTR = 16
PAIRS = 16
GW = 24
ETILES = FE // P
DENSE_AT = NE * ETILES
FFCOLS = 2 * D + D
SLOT = FFCOLS + 8


class Line:

    alone = None

    def __init__(self, nc, name, eng=None, step=1):
        self.nc, self.eng, self.step = nc, eng, step
        self.sem = nc.alloc_semaphore(name)
        self.reset()

    def reset(self):
        self.count, self.terms, self.seen = 0, (), {}

    def wait(self, *marks):
        for line, value, terms in marks:
            key = (line, terms)
            if self.seen.get(key, 0) >= value:
                continue
            self.seen[key] = value
            for loop, per_turn in terms:
                value = loop.index * per_turn + value
            self.eng.wait_ge(line.sem, value)
            if self.alone is not None and terms:
                self.eng.sem_inc(self.alone, 1)

    def mark(self, inst):
        inst.then_inc(self.sem, self.step)
        self.count += self.step
        return (self, self.count, self.terms)

    def __call__(self, marks, fn, *args, **kw):
        self.wait(*marks)
        return self.mark(fn(*args, **kw))

    def now(self):
        return (self, self.count, self.terms)

    def at(self, n):
        return (self, self.count + n * self.step, self.terms)


class Turns:

    met = None

    def __init__(self, nc, n, lines, per):
        self.nc, self.n, self.lines, self.per = nc, n, lines, per
        self.fori = nc.Fori(0, n)

    def __enter__(self):
        if any(q.terms for q in self.lines):
            for q in {q.eng: q for q in self.lines if q.eng is not None}.values():
                q.eng.sem_inc(self.met, 1)
        i = self.index = self.fori.__enter__()
        self.start = {q: q.count for q in self.lines}
        for q in self.lines:
            k = self.per.get(q, 0)
            q.terms += ((self, k),) if k else ()
            q.seen = {}
        return i

    def __exit__(self, *exc):
        for q in self.lines:
            k = self.per.get(q, 0)
            if exc[0] is None:
                assert q.count - self.start[q] == k, (q.sem.name, q.count - self.start[q], k)
            q.count = self.start[q] + self.n * k
            q.terms = q.terms[:-1] if k else q.terms
            q.seen = {}
        return self.fori.__exit__(*exc)


def before(mark):
    line, value, terms = mark
    assert value - terms[-1][1] > 0, (line.sem.name, value, terms)
    return (line, value - terms[-1][1], terms)


class Bank:

    def __init__(self, ap):
        self.ap, self.free = ap, ()


class Ring:

    def __init__(self, nc, sp, W, lines, split):
        self.nc, self.sp, self.W, self.lines, self.split = nc, sp, W, lines, split
        self.reset()

    def reset(self, slot_free=(), parts_free=()):
        self.free = [slot_free] * len(self.lines)
        self.parts_free = [parts_free] * 2
        self.sources, self.arrival, self.ready = [], {}, {}
        self.loaded = self.released = self.taken = 0

    def plan(self, sources, raw=False):
        self.sources += [(s, raw) for s in sources]
        self._fill()

    def _fill(self):
        n = len(self.lines)
        while self.loaded < len(self.sources) and self.loaded < self.released + n:
            k = self.loaded % n
            src = self.sources[self.loaded][0]
            self.sp.wait(*self.free[k])
            self.arrival[self.loaded] = self.lines[k].mark(
                self.nc.sync.dma_start(self.W[:, k, 0:src.shape[-1]], src))
            self.loaded += 1

    def _split(self, c):
        if c < len(self.sources) and not self.sources[c][1] and c not in self.ready:
            k = c % len(self.lines)
            width = self.sources[c][0].shape[-1]
            parity = c % 2
            made, read = self.split(self.W[:, k, :], width, parity, (self.arrival[c],), self.parts_free[parity])
            self.free[k] = read
            self.ready[c] = (parity, made)
            self.released = c + 1
            self._fill()

    def prepare(self):
        self._split(self.taken)

    def take(self):
        c = self.taken
        self._split(c)
        self.taken += 1
        return self.ready[c]

    def taken_by(self, mark):
        self.parts_free[(self.taken - 1) % 2] = (mark,)
        self._split(self.taken)

    def take_raw(self):
        c = self.taken
        self.taken += 1
        return self.W[:, c % len(self.lines), :], self.arrival[c]

    def taken_raw_by(self, mark):
        self.free[(self.taken - 1) % len(self.lines)] = (mark,)
        self.released = self.taken
        self._fill()
        self._split(self.taken)


def program(nc, dr, out):
    vec, act_e, pe_e, pool_e, sync = nc.vector, nc.scalar, nc.tensor, nc.gpsimd, nc.sync
    V = Line(nc, "vector_done", vec)
    A = Line(nc, "scalar_done", act_e)
    T = Line(nc, "tensor_done", pe_e)
    G = Line(nc, "gpsimd_done", pool_e)
    SP = Line(nc, "sync_done", sync)
    Turns.met = nc.alloc_semaphore("loop_entered")
    SP.alone = Turns.met
    AS = Line(nc, "high_part_split", act_e)
    VS = Line(nc, "low_part_split", vec)
    GS = Line(nc, "low_part_split_gpsimd", pool_e)
    TF = Line(nc, "ff_tensor_done", pe_e)
    VF = Line(nc, "ff_vector_done", vec)
    AF = Line(nc, "ff_scalar_done", act_e)
    VG = Line(nc, "gather_vector_done", vec)
    slots = [Line(nc, f"slot{k}_loaded", step=16) for k in range(TURN)]
    down_slots = [Line(nc, f"down_slot{k}_loaded", step=16) for k in range(TURN)]
    const_in = Line(nc, "first_constants_loaded", step=16)
    tables_in = Line(nc, "tables_loaded", step=16)
    SEEDED = (TF, VF, AF, AS, VS, GS)
    mem_in = Line(nc, "memory_loaded", step=16)
    columns_in = Line(nc, "layer_columns_loaded", step=16)
    layer_in = Line(nc, "layer_loaded", step=16)
    stored = Line(nc, "result_stored", step=16)
    lines = [V, A, T, G, SP, AS, VS, GS, TF, VF, AF, VG, *slots, *down_slots, const_in, tables_in, mem_in, columns_in,
             layer_in]

    def seed():
        for q in SEEDED:
            q.eng.sem_inc(q.sem, 64)
            q.count += 64

    seed()

    def sb(name, shape, dt=F32):
        return nc.alloc_sbuf_tensor(name, shape, dt)

    X = sb("residual", [P, TT, D])
    HT = sb("hidden_columns", [P, KT, S])
    XN = sb("normalised_rows", [P, TT, D])
    DUMMY = sb("nothing", [P, 1])[:, :]
    HH = sb("hidden_columns_high", [P, KT, S], F32R)
    HL = sb("hidden_columns_low", [P, KT, S], F32R)
    KVB = sb("memory_keys_values_b", [P, 4, S])
    WH = sb("weights_high", [P, 2, 2 * D], F32R)
    WL = sb("weights_low", [P, 2, 2 * D], F32R)
    DH = sb("down_weights_high", [P, 2, D], F32R)
    DL = sb("down_weights_low", [P, 2, D], F32R)
    W = sb("weight_ring", [P, TURN, SLOT])
    AH = sb("gated_columns_high", [P, 2, S], F32R)
    AL = sb("gated_columns_low", [P, 2, S], F32R)
    GC = sb("gated_columns", [P, 2, S])
    SG = sb("silu_columns", [P, 2, S])
    IDENT = sb("identity", [P, P])
    DIST = sb("distance", [P, 384])
    CAUS = sb("causal", [P, 384])
    LEVEL = sb("level_masks", [P, 8, P], U8)
    RESET = sb("chunk_reset", [P, S])
    TRIL = sb("keep_lower", [P, P])
    ROPE = sb("rope", [P, TT, 16])
    CROPE = sb("rope_compressed", [NC, 16])
    CMPA = sb("compressed_mask_add", [P, TT, NC])
    CMPK = sb("compressed_mask_keep", [P, TT, NC])
    IOTA = sb("expert_numbers", [P, NE])
    PLACE = sb("place_numbers", [P, CAP])
    ONES = sb("ones", [P, P])
    GAINS = sb("gains", [P, 7, KT])
    SMALL = sb("small_parameters", [P, 10])
    LBL = sb("bound_logits", [P, HEADS])
    ROUT = sb("router", [P, KT, NE])
    FING = sb("row_gain", [P, D])
    ST = sb("statistics", [P, 160])
    STI = sb("indices", [P, 16], U32)
    ARENA = sb("arena", [P, 11264])
    PS = nc.alloc_psum_tensor("banks", [P, 8, 512], F32)
    banks = [Bank(PS[:, b, :]) for b in range(8)]

    def f32(ap):
        return ap.bitcast(F32)

    def split_part(raw, high, low, n, share, arrived, free):
        AS.wait(*arrived)
        VS.wait(*arrived)
        h = AS(free, act_e.copy, high[:, 0:n], raw[:, 0:n])
        v = VS((h, *free), vec.tensor_tensor, low[:, 0:n - share], raw[:, 0:n - share], f32(high[:, 0:n - share]),
               ALU.subtract)
        if not share:
            return (h, v)
        GS.wait(*arrived)
        g = GS((h, *free), pool_e.tensor_tensor, low[:, n - share:n], raw[:, n - share:n],
               f32(high[:, n - share:n]), ALU.subtract)
        return (h, v, g)

    def split_chunk(raw, width, parity, arrived, free):
        made = split_part(raw, WH[:, parity, :], WL[:, parity, :], width, 0, arrived, free)
        return made, made

    ring = Ring(nc, SP, W, slots, split_chunk)

    def product(to, lh, ll, rh, rl, first, last):
        pe_e.matmul(to, lh, rh, start=first, stop=False)
        pe_e.matmul(to, lh, rl, start=False, stop=False)
        return pe_e.matmul(to, ll, rh, start=False, stop=last)

    used = [0]

    def room(*shape):
        n = int(np.prod(shape))
        a, used[0] = used[0], used[0] + n
        assert used[0] <= 11264, used[0]
        ap = ARENA[:, a:a + n]
        if len(shape) == 2:
            ap = ap.rearrange("p (a b) -> p a b", a=shape[0])
        if len(shape) == 3:
            ap = ap.rearrange("p (a b c) -> p a b c", a=shape[0], b=shape[1])
        return ap

    stat_used = [0]

    def stat(n=1):
        if stat_used[0] + n > 160:
            stat_used[0] = 0
        a = stat_used[0]
        stat_used[0] += n
        return ST[:, a:a + n]

    def spread(ap, n):
        return ap.unsqueeze(2).broadcast_to([ap.shape[0], ap.shape[1], n])


    def root(ssq, n, width, ready):
        m = V(ready, vec.tensor_scalar, ssq, ssq, 1.0 / width, EPS, ALU.mult, ALU.add)
        m = A((m,), act_e.activation, ssq, ssq, ACT.Sqrt)
        return V((m,), vec.reciprocal, ssq, ssq)

    def turn(src, n, gain, dst, ready, free=()):
        marks, k = [], 0
        for t in range(TT):
            for c0 in range(0, n, 4):
                w = min(4, n - c0)
                bank = banks[4 + k % 4]
                k += 1
                T.wait(*ready, *bank.free)
                for c in range(w):
                    last = pe_e.transpose(bank.ap[:, c * P:(c + 1) * P], src(t, c0 + c), IDENT[:, :])
                turned = T.mark(last)
                seen = bank.ap[:, 0:w * P].rearrange("p (c t) -> p c t", c=w)
                to = dst[:, c0:c0 + w, t * P:(t + 1) * P]
                if gain is None:
                    m = A((turned, *free), act_e.copy, to, seen)
                else:
                    m = V((turned, *free), vec.tensor_tensor, to, seen, spread(gain[:, c0:c0 + w], P), ALU.mult)
                bank.free = (m,)
                if dst is HT:
                    at = (slice(None), slice(c0, c0 + w), slice(t * P, (t + 1) * P))
                    h = A((m, *free), act_e.copy, HH[at], to)
                    marks.append(h)
                    m = V((h, *free), vec.tensor_tensor, HL[at], to, f32(HH[at]), ALU.subtract)
                marks.append(m)
        return tuple(marks[-8:])

    def rms_scale(src, dst, width, ready, free=()):
        ssq = stat(TT)
        marks = []
        for t in range(TT):
            marks.append(A((*ready, *free), act_e.activation, dst[:, t, :], src[:, t, :], ACT.Square,
                           accum_out=ssq[:, t:t + 1]))
        r = root(ssq, TT, width, tuple(marks))
        return (A((r,), act_e.activation, dst[:, 0, :], src[:, 0, :], ACT.Copy, scale=ssq[:, 0:1]),
                V((r,), vec.tensor_scalar, dst[:, 1, :], src[:, 1, :], ssq[:, 1:2], None, ALU.mult))

    def norm_columns(src, gain, dst, ready, free=()):
        m = rms_scale(src, XN, D, ready, (T.now(), V.now()))
        ring.prepare()
        return turn(lambda t, c: XN[:, t, c * P:(c + 1) * P], KT, gain, dst, m, free)

    bank_turn = [0]

    def next_bank():
        bank_turn[0] += 1
        return banks[4 + bank_turn[0] % 4]

    def project(n, ready, evac, form, kt=KT):
        out_marks = []
        for c in range(n):
            parity, made = ring.take()
            wh, wl = (x[:, parity, :].rearrange("p (k n) -> p k n", k=kt) for x in (WH, WL))
            bank = next_bank()
            T.wait(*made, *ready, *bank.free)
            for s in range(2):
                for i in range(kt):
                    cut = slice(s * P, (s + 1) * P)
                    if form == "rows":
                        ops = HH[:, i, cut], HL[:, i, cut], wh[:, i, :], wl[:, i, :]
                    else:
                        ops = wh[:, i, cut], wl[:, i, cut], HH[:, i, :], HL[:, i, :]
                    last = product(bank.ap[:, s * 256:(s + 1) * 256], *ops, i == 0, i == kt - 1)
            m = T.mark(last)
            ring.taken_by(m)
            bank.free = evac(c, bank.ap.rearrange("p (s n) -> p s n", s=2), m)
            out_marks += bank.free
        return tuple(out_marks)

    def copy_to(dst, scale=1.0, func=ACT.Copy):
        def go(c, seen, m):
            return (A((m,), act_e.activation, dst[:, 2 * c:2 * c + 2, :], seen, func, scale=scale),)
        return go

    def copy_rows(dst, scale=1.0, func=ACT.Copy):
        def go(c, seen, m):
            return (A((m,), act_e.activation, dst[:, :, c * 256:(c + 1) * 256], seen, func, scale=scale),)
        return go

    def add_rows(dst):
        def go(c, seen, m):
            part = dst[:, :, c * 256:(c + 1) * 256]
            return (V((m,), vec.tensor_tensor, part, part, seen, ALU.add),)
        return go

    TRI = [(0, P, 0), (1, S, P)]
    FULL = [(0, S, 0), (1, S, S)]

    def attend(heads, segs, q_of, k_of, v_of, prepare, finish, ready, bufs, vw, keys=P, keep=None, maps=1):
        ncol = max(c + n for _, n, c in segs)
        P_, PT = bufs
        state = {}

        def scores(h):
            got = []
            for m in range(maps):
                bank = banks[(h * maps + m) % 4]
                T.wait(*ready, *bank.free)
                for q, n, c in segs:
                    last = pe_e.matmul(bank.ap[:, c:c + n], q_of(h, m, q), k_of(h, m, n), start=True, stop=True)
                got.append((bank, T.mark(last)))
            state[h] = got

        def soften(h):
            ps = P_[h % 2]
            res = []
            for m, (bank, made) in enumerate(state[h]):
                raw = bank.ap[:, 0:ncol]
                mine = ps[:, m, 0:ncol]
                free = state.get(("turned", h - 2), ())
                if prepare is None:
                    V.wait(made, *free)
                    ready_s, from_ = made, raw
                else:
                    ready_s = prepare(h, mine, raw, (made, *free))
                    from_ = mine
                top, tot = stat(2), stat(2)
                if segs == FULL:
                    mx = V((ready_s,), vec.tensor_reduce, top, from_.rearrange("p (s n) -> p s n", s=2), AX_X,
                           ALU.max, negate=True)
                else:
                    for i, (q, n, c) in enumerate(segs):
                        mx = V((ready_s,), vec.tensor_reduce, top[:, i:i + 1], from_[:, c:c + n], AX_X, ALU.max,
                               negate=True)
                for i, (q, n, c) in enumerate(segs):
                    e = A((mx, *free), act_e.activation, mine[:, c:c + n], from_[:, c:c + n], ACT.Exp,
                          bias=top[:, i:i + 1], accum_out=tot[:, i:i + 1])
                bank.free = (e, mx)
                res.append((tot, e))
            if maps == 2:
                (t0, e0), (t1, e1) = res
                r = V((e0, e1), vec.reciprocal, t0, t0)
                V((), vec.reciprocal, t1, t1)
                r = V((V.now(),), vec.tensor_scalar, t1, t1, LAM, None, ALU.mult)
                for i, (q, n, c) in enumerate(segs):
                    V((r,), vec.tensor_scalar, ps[:, 1, c:c + n], ps[:, 1, c:c + n], t1[:, i:i + 1], None, ALU.mult)
                sub = V.now()
                for i, (q, n, c) in enumerate(segs):
                    e = V((sub,), vec.scalar_tensor_tensor, ps[:, 0, c:c + n], ps[:, 0, c:c + n], t0[:, i:i + 1],
                          ps[:, 1, c:c + n], ALU.mult, ALU.subtract)
                state["p", h] = (None, e)
            else:
                tot, e = res[0]
                if keep is not None:
                    e = V((e,), vec.tensor_tensor, ps[:, 0, 0:ncol], ps[:, 0, 0:ncol], keep, ALU.mult)
                    e = V((e,), vec.tensor_reduce, tot, ps[:, 0, 0:ncol].rearrange("p (s n) -> p s n", s=2), AX_X,
                          ALU.add)
                    e = V((e,), vec.tensor_scalar, tot, tot, 1e-30, None, ALU.max)
                e = V((e,), vec.reciprocal, tot, tot)
                state["p", h] = (tot, e)

        def turn_p(h):
            tot, e = state["p", h]
            ps, pt = P_[h % 2], PT[h % 2]
            bank = banks[4 + h % 2]
            T.wait(e, *bank.free)
            col = 0
            for q, n, c in segs:
                for k0 in range(0, n, keys):
                    last = pe_e.transpose(bank.ap[0:keys, col:col + P], ps[:, 0, c + k0:c + k0 + keys], IDENT[:, :])
                    col += P
            m = T.mark(last)
            state["turned", h] = (m,)
            cp = V if h % 2 else A
            fn = vec.tensor_copy if h % 2 else act_e.copy
            got = cp((m, *state.get(("used", h - 2), ())), fn, pt[0:keys, 0:col], bank.ap[0:keys, 0:col])
            bank.free = (got,)
            state["pt", h] = got

        def values(h):
            tot, _ = state["p", h]
            pt = PT[h % 2]
            bank = banks[6 + h % 2]
            T.wait(state["pt", h], *bank.free)
            col = 0
            for q, n, c in segs:
                kts = range(0, n, keys)
                for i in kts:
                    last = pe_e.matmul(bank.ap[:, q * vw:(q + 1) * vw], pt[0:keys, col:col + P], v_of(h, i // keys),
                                       start=i == 0, stop=i == kts[-1])
                    col += P
            m = T.mark(last)
            state["used", h] = (m,)
            bank.free = (finish(h, bank.ap[:, 0:2 * vw].rearrange("p (s n) -> p s n", s=2), tot, m),)

        for s in range(heads + 2):
            if s < heads:
                scores(s)
                soften(s)
            if 1 <= s <= heads:
                turn_p(s - 1)
            if s >= 2:
                values(s - 2)
        return (V.now(), A.now())


    used[0] = 0
    KVA = room(4, S)
    MT = room(KT, S)
    LEVEL4 = room(8, P).bitcast(I32)
    mem_in.mark(act_e.dma_start(XN[:], dr["mem"]))
    for dst, name in ((IDENT, "ident"), (GAINS, "gains"), (SMALL, "small"), (LBL, "b_lb_logits")):
        const_in.mark(act_e.dma_start(dst[:], dr[name]))
    consts = const_in.now()
    ring.plan([dr[w][c] for w in ("a_w_mem_kv", "b_w_mem_kv") for c in range(2)]
              + [dr["a_w_in"][c] for c in range(10)] + [dr["a_w_out"][c] for c in range(4)])
    A.wait(V((), vec.memset, DUMMY, 0.0))
    ones = V((), vec.memset, ONES[:, :], 1.0)
    for q in (V, A, T, G):
        q.wait(consts)

    g_amix, g_amem, g_bmix, g_bmem, g_dense, g_moe = (GAINS[:, i, :] for i in range(6))

    LAM = sb("lambda", [P, 1])[:, :]
    prod = stat(2)
    z = V((), vec.memset, prod, 0.0)
    z = V((z,), vec.tensor_tensor, prod[0:64, 0:1], SMALL[0:64, 4:5], SMALL[0:64, 5:6], ALU.mult)
    z = V((), vec.tensor_tensor, prod[0:64, 1:2], SMALL[0:64, 6:7], SMALL[0:64, 7:8], ALU.mult)
    m = T((z, ones), pe_e.matmul, banks[0].ap[:, 0:2], ONES[:, :], prod, start=True, stop=True)
    e2 = stat(2)
    m = A((m,), act_e.activation, e2, banks[0].ap[:, 0:2], ACT.Exp)
    banks[0].free = (m,)
    m = V((m,), vec.tensor_tensor, LAM, e2[:, 0:1], e2[:, 1:2], ALU.subtract)
    lam_ready = V((m,), vec.tensor_scalar, LAM, LAM, LAM_INIT, None, ALU.add)
    GA = sb("gain_a", [P, KT])[:, :]
    GB = sb("gain_b", [P, KT])[:, :]
    m = V((), vec.memset, GA, 1.0)
    m = V((m,), vec.memset, GB, 1.0)
    V((m,), vec.tensor_scalar, GA[:, 0:HEADS], GA[:, 0:HEADS], SMALL[:, 0:1], 1.0 - LAM_INIT, ALU.mult, ALU.mult)
    V((m,), vec.tensor_scalar, GB[:, 0:HEADS], GB[:, 0:HEADS], SMALL[:, 1:2], None, ALU.mult)
    LB = sb("bound", [P, HEADS])[:, :]
    OMLB = sb("one_less_bound", [P, HEADS])[:, :]
    m = V((), vec.tensor_tensor, LB, LBL[:, :], LBL[:, :], ALU.subtract)
    m = A((m,), act_e.activation, LB, LB, ACT.Exp)
    m = V((m,), vec.reciprocal, OMLB, LB)
    m = V((m,), vec.tensor_tensor, OMLB, OMLB, LB, ALU.mult)
    m = V((m,), vec.tensor_tensor, LB, OMLB, OMLB, ALU.subtract)
    lb_ready = V((m,), vec.tensor_scalar, OMLB, LB, -1.0, 1.0, ALU.mult, ALU.add)

    m = tuple(A((mem_in.now(),), act_e.activation, HT[:, 4 * t:4 * t + 4, :].rearrange("p a b -> p (a b)"),
                XN[:, t, :], ACT.Square, accum_out=ST[:, 150 + t:151 + t]) for t in range(TT))
    r = root(ST[:, 150:152], TT, D, m)
    m = tuple(A((r,), act_e.activation, XN[:, t, :], XN[:, t, :], ACT.Copy, scale=ST[:, 150 + t:151 + t])
              for t in range(TT))
    memory_ready = turn(lambda t, c: XN[:, t, c * P:(c + 1) * P], KT, None, MT, m, m)
    memory_kv = []
    for dst, name in ((X[:], "x"), (DIST[:], "dist"), (LEVEL4, "levels"), (CAUS[:], "causal"), (RESET[:], "reset"),
                      (TRIL[:], "tri"), (ROPE[:], "rope"), (CROPE[:], "crope"), (CMPA[:], "cmp_add"),
                      (CMPK[:], "cmp_keep"), (IOTA[:], "iota"), (PLACE[:], "place"), (ROUT[:], "moe_router")):
        tables_in.mark(act_e.dma_start(dst, dr[name]))
    for gain, kv in ((g_amem, KVA), (g_bmem, KVB[:, :, :])):
        gm = V((*memory_ready, T.now(), A.now(), V.now()), vec.tensor_tensor, HT[:, :, :], MT, spread(gain, S),
               ALU.mult)
        gh = A((gm, T.now()), act_e.copy, HH[:, :, :], HT[:, :, :])
        gl = V((gh, T.now()), vec.tensor_tensor, HL[:, :, :], HT[:, :, :], f32(HH[:, :, :]), ALU.subtract)
        mk = project(1, (gh, gl), copy_to(kv[:, 0:2, :]), "columns")
        memory_kv += [*mk, *project(1, (gh, gl), copy_rows(kv[:, 2:4, :]), "rows")]

    def mixer_memory(kv, qm, O, ready, bufs):
        kT, v = kv[:, 0:2, :], kv[:, 2:4, :]

        def rows_of(h):
            return slice(64 * (h % 2), 64 * (h % 2) + 64)

        def finish(h, seen, tot, m):
            return V((m,), vec.tensor_tensor, O[:, :, 768 + h * HD:768 + (h + 1) * HD], seen, spread(tot, HD),
                     ALU.mult)

        return attend(MEM_HEADS, FULL, lambda h, m, q: qm[rows_of(h), h // 2, q * P:(q + 1) * P],
                      lambda h, m, n: kT[rows_of(h), h // 2, 0:n], lambda h, i: v[:, i, h * HD:(h + 1) * HD],
                      None, finish, (*memory_kv, *ready), bufs, HD)

    def head_norm(O, ready):
        heads = O[:, :, 0:768]
        ssq = stat(TT * HEADS)
        for t in range(TT):
            sq = A(ready, act_e.activation, XN[:, t, 0:768], heads[:, t, :], ACT.Square)
        sq = V((sq,), vec.tensor_reduce, ssq.rearrange("p (t h) -> p t h", t=TT),
               XN[:, :, 0:768].rearrange("p t (h e) -> p t h e", h=HEADS), AX_X, ALU.add)
        r = root(ssq, 12, P, (sq,))
        for t in range(TT):
            part = heads[:, t, :].rearrange("p (h e) -> p h e", h=HEADS)
            r2 = V((r,), vec.tensor_tensor, part, part, spread(ssq[:, t * HEADS:(t + 1) * HEADS], P), ALU.mult)
        return r2


    for q in (V, A, T, G):
        q.wait(tables_in.now())
    levels_ready = V((), vec.tensor_copy, LEVEL[:, :, :], LEVEL4)
    h_ready = norm_columns(X, g_amix, HT, (), (*memory_ready, *memory_kv, T.now(), levels_ready))
    used[0] = 4 * S
    qT, kT, v, qm = room(HEADS, S), room(HEADS, S), room(TT, 768), room(2, S)
    O = room(TT, D)
    mq = project(3, h_ready, copy_to(qT, HD ** -0.5), "columns")
    mk = project(3, h_ready, copy_to(kT), "columns")
    mv = project(3, h_ready, copy_rows(v), "rows")
    mm = project(1, h_ready, copy_to(qm, HD ** -0.5), "columns")
    p_bufs = [room(2, 512), room(2, 512)], [room(512), room(512)]

    def half(m):
        return slice(64 * m, 64 * m + 64)

    def with_distance(h, mine, raw, ready):
        return V(ready, vec.scalar_tensor_tensor, mine, DIST[:, :], -SLOPES[h], raw, ALU.mult, ALU.add)

    def diff_out(h, seen, tot, m):
        return A((m,), act_e.copy, O[:, :, h * P:(h + 1) * P], seen)

    V.wait(lam_ready)
    done = attend(HEADS, TRI, lambda h, m, q: qT[half(m), h, q * P:(q + 1) * P],
                  lambda h, m, n: kT[half(m), h, 0:n], lambda h, i: v[:, i, h * P:(h + 1) * P],
                  with_distance, diff_out, (*mq, *mk, *mv), p_bufs, P, maps=2)
    normed = head_norm(O, done)
    done = mixer_memory(KVA, qm, O, mm, p_bufs)
    o_ready = turn(lambda t, c: O[:, t, c * P:(c + 1) * P], KT, GA, HT, (*done, normed), (T.now(),))
    x_ready = project(4, o_ready, add_rows(X), "rows")


    def start_anew():
        nc.all_engine_barrier()
        for q in lines:
            pool_e.sem_clear(q.sem)
            q.reset()
        nc.all_engine_barrier()
        ring.reset()
        for b in banks:
            b.free = ()
        seed()

    class Swiglu:
        vector_ops, scalar_ops = 3, 1

        def __call__(self, ff, j, gate, up, made):
            w, b = ff.width, j % 2
            a = AF((made, ff.tile_done(j - 2)), act_e.activation, SG[:, b, 0:w], gate, ACT.Silu)
            return self.parts(ff, j, a, SG[:, b, 0:w], up, ())

        def parts(self, ff, j, a, one, other, ready):
            w, b = ff.width, j % 2
            v = VF((a, *ready, ff.tile_done(j - 2)), vec.tensor_tensor, GC[:, b, 0:w], one, other, ALU.mult)
            v = VF((v, ff.down_done(j - 2)), vec.tensor_copy, AH[:, b, 0:w], GC[:, b, 0:w])
            return VF((v,), vec.tensor_tensor, AL[:, b, 0:w], GC[:, b, 0:w], f32(AH[:, b, 0:w]), ALU.subtract)

    class Conv(Swiglu):
        vector_ops, scalar_ops = 9, 1

        def __call__(self, ff, j, gate, up, made):
            c = W[:, j % TURN, FFCOLS:FFCOLS + 8]
            VF.wait(made, ff.tile_done(j - 1))
            done = []
            for i, src in enumerate((gate, up)):
                k, buf = c[:, 4 * i:4 * i + 4], CV[:, i, :]
                v = VF((), vec.tensor_scalar, buf, src, k[:, 2:3], k[:, 3:4], ALU.mult, ALU.add)
                v = VF((v,), vec.scalar_tensor_tensor, buf[:, 1:S], src[:, 0:S - 1], k[:, 1:2], buf[:, 1:S],
                       ALU.mult, ALU.add)
                done.append(VF((v,), vec.scalar_tensor_tensor, buf[:, 2:S], src[:, 0:S - 2], k[:, 0:1],
                               buf[:, 2:S], ALU.mult, ALU.add))
            a = AF((done[0], ff.tile_done(j - 2)), act_e.activation, SG[:, j % 2, :], CV[:, 0, :], ACT.Silu)
            return self.parts(ff, j, a, SG[:, j % 2, :], CV[:, 1, :], (done[1],))

    class Chunks:

        def __init__(self, ap, first, width=FFCOLS):
            self.ap, self.first, self.width = ap, first, width

        def __call__(self, n):
            at = self.first + n
            if isinstance(at, int):
                return self.ap[at]
            return self.ap[bass.ds(at, 1)].rearrange("o p n -> (o p) n")

    def fold_rows(dst):
        def go(m):
            for t in range(TT):
                VF((m,), vec.tensor_tensor, dst[:, t, :], dst[:, t, :],
                   PS[:, 2 * t:2 * t + 2, :].rearrange("p a b -> p (a b)"), ALU.add)
        go.ops = TT
        return go

    class FeedForward:

        def __init__(self, chunks, width, gate_tile, fold):
            self.chunks, self.width, self.gate_tile, self.fold = chunks, width, gate_tile, fold
            v = gate_tile.vector_ops
            self.turn_sizes = (TURN,)
            self.places = {"gate_up": (TF, lambda j, n: 2 * j if j else 1),
                           "down": (TF, lambda j, n: 2 * j + 3 if j < n - 1 else 2 * n),
                           "tile": (VF, lambda j, n: v * (j + 1)),
                           "split_gate_up": (VS, lambda j, n: 2 * j - 1),
                           "split_down": (VS, lambda j, n: 2 * j + 2),
                           "split_gate_up_gpsimd": (GS, lambda j, n: j if j else n)}

        def per(self, n):
            g = self.gate_tile
            return {TF: 2 * n, VF: g.vector_ops * n + self.fold.ops, AF: g.scalar_ops * n + 1, VS: 2 * n, AS: 2 * n,
                    GS: n, **{q: 16 * n // TURN for q in (*slots, *down_slots)}}

        def at(self, kind, j):
            if j >= 0:
                return self.marks[kind, j]
            line, place = self.places[kind]
            back = min(self.per(n)[line] - place(j + n, n) for n in self.turn_sizes)
            return (line, self.start[line] - back, line.terms)

        def tile_done(self, j):
            return self.at("tile", j)

        def down_done(self, j):
            return self.at("down", j)

        def begin(self, first=0):
            SP.wait(*[m for marks in ring.free for m in marks])
            self.load(0, first)
            self.load_down(0, first)
            for q in (VS, AS, GS):
                q.wait(*ring.parts_free[0], *ring.parts_free[1])
            self.split_gate_up(0, slots[0].now(), ())

        def load(self, j, tile):
            slots[j % TURN].mark(sync.dma_start(W[:, j % TURN, 0:2 * D], self.chunks(tile)[:, 0:2 * D]))

        def load_down(self, j, tile):
            n = self.chunks.width
            down_slots[j % TURN].mark(sync.dma_start(W[:, j % TURN, 2 * D:n], self.chunks(tile)[:, 2 * D:n]))

        def load_next(self, j, first, split):
            tile = first + j + 1
            if not isinstance(tile, int):
                tile = sync.snap(tile)
            old = j + 1 - TURN
            SP.wait(self.at("split_gate_up", old) if old < 0 else split[0][0],
                    self.at("split_gate_up_gpsimd", old) if old < 0 else split[0][1])
            self.load(j + 1, tile)
            SP.wait(self.at("split_down", old), self.tile_done(old))
            self.load_down(j + 1, tile)
            split[j + 1] = self.split_gate_up(j + 1, slots[(j + 1) % TURN].now(), (self.at("gate_up", j - 1),))
            self.down_arrival[j + 1] = down_slots[(j + 1) % TURN].now()
            self.marks["split_gate_up", j + 1] = split[j + 1][1]
            self.marks["split_gate_up_gpsimd", j + 1] = split[j + 1][2]

        def split_gate_up(self, j, arrived, free):
            return split_part(W[:, j % TURN, 0:2 * D], WH[:, j % 2, :], WL[:, j % 2, :], 2 * D, POOL_SHARE,
                              (arrived,), free)

        def split_down(self, j, free):
            return split_part(W[:, j % TURN, 2 * D:3 * D], DH[:, j % 2, :], DL[:, j % 2, :], D, 0,
                              (self.down_arrival[j],), free)[1]

        def tiles(self, n, first, more):
            self.n, self.marks = n, {}
            self.start = {q: q.count for q in (TF, VF, VS, GS)}
            split, self.down_arrival = {0: (VS.now(), GS.now())}, {0: down_slots[0].now()}
            AF((), act_e.activation, DUMMY, DUMMY, ACT.Silu)
            for j in range(n):
                if j + 1 < n or more:
                    self.load_next(j, first, split)
                self.marks["split_down", j] = self.split_down(j, (self.down_done(j - 2),))
                self.gate_up(j, split[j])
                if j:
                    self.down(j - 1)
            self.down(n - 1)
            self.fold(TF.now())

        def gate_up(self, j, split):
            w = self.width
            bank = banks[4 + j % 2]
            wh, wl = (x[:, j % 2, :].rearrange("p (k n) -> p k n", k=KT) for x in (WH, WL))
            TF.wait(*split, self.tile_done(j - 2))
            for h in range(2):
                for i in range(KT):
                    last = product(bank.ap[:, h * 256:h * 256 + w], wh[:, i, h * P:(h + 1) * P],
                                   wl[:, i, h * P:(h + 1) * P], HH[:, i, 0:w], HL[:, i, 0:w], i == 0, i == KT - 1)
            made = self.marks["gate_up", j] = TF.mark(last)
            self.marks["tile", j] = self.gate_tile(self, j, bank.ap[:, 0:w], bank.ap[:, 256:256 + w], made)

        def down(self, j):
            TF.wait(self.at("split_down", j), self.tile_done(j))
            if j == 0:
                TF.wait((VF, self.start[VF], VF.terms))
            for t in range(self.width // P):
                cut = slice(t * P, (t + 1) * P)
                for h in range(2):
                    cols = slice(h * 512, (h + 1) * 512)
                    last = product(banks[2 * t + h].ap, AH[:, j % 2, cut], AL[:, j % 2, cut], DH[:, j % 2, cols],
                                   DL[:, j % 2, cols], j == 0, j == self.n - 1)
            self.marks["down", j] = TF.mark(last)

        def turns(self, n, first=0):
            size = self.turn_sizes[0]
            with Turns(nc, n, lines, self.per(size)) as i:
                self.tiles(size, first + i * size, True)

        def run(self, tiles, ready):
            TF.wait(*ready)
            VF.wait(*ready)
            for b in banks:
                TF.wait(*b.free)
            self.turns(tiles // TURN)
            if tiles % TURN:
                self.tiles(tiles % TURN, tiles // TURN * TURN, False)
            return self.end()

        def end(self):
            done = TF.now(), VF.now(), AF.now(), VS.now(), AS.now(), GS.now()
            for b in banks:
                b.free = done
            ring.reset((VS.now(), GS.now(), VF.now()), (TF.now(),))
            return done

    class GatheredFeedForward(FeedForward):

        def __init__(self, chunks, fold):
            super().__init__(chunks, CAP, Swiglu(), fold)
            self.turn_sizes = (2 * TURN, ETILES % (2 * TURN))
            self.places.update({
                "gate_up": (TF, lambda j, n: (1, 2)[j] if j < 2 else 3 * j - 2),
                "turned": (TF, lambda j, n: 3 if j == 0 else 3 * j + 2 if j < n - 1 else 3 * n - 2),
                "down": (TF, lambda j, n: 3 * j + 6 if j < n - 2 else 3 * n - (n - 1 - j)),
                "multiplied": (VF, lambda j, n: 2 * j if j else 1),
                "tile": (VF, lambda j, n: 2 * j + 3 if j < n - 1 else 2 * n),
                "split_gate_up": (VS, lambda j, n: j if j < 2 else 2 * j - 2),
                "split_down": (VS, lambda j, n: 2 * j + 3 if j < n - 1 else 2 * n)})

        def per(self, n):
            return {**super().per(n), TF: 3 * n, VF: 2 * n + self.fold.ops, AF: 2 * n + 1}

        def expert(self, first):
            size, rest = self.turn_sizes
            self.turns(ETILES // size, first)
            self.tiles(rest, first + ETILES - rest, True)

        def expert_counts(self):
            size, rest = self.turn_sizes
            inner = self.per(size)
            return {q: ETILES // size * inner[q] + k for q, k in self.per(rest).items()}

        def tiles(self, n, first, more):
            self.n, self.marks = n, {}
            self.start = {q: q.count for q in (TF, VF, VS, GS)}
            split, self.down_arrival = {0: (VS.now(), GS.now())}, {0: down_slots[0].now()}
            AF((), act_e.activation, DUMMY, DUMMY, ACT.Silu)
            for j in range(n):
                self.load_next(j, first, split)
                if j:
                    self.marks["split_down", j - 1] = self.split_down(j - 1, (self.down_done(j - 3),))
                self.gate_up(j, split[j])
                if j:
                    self.turn_tile(j - 1)
                if j > 1:
                    self.down(j - 2)
            self.marks["split_down", n - 1] = self.split_down(n - 1, (self.down_done(n - 3),))
            self.turn_tile(n - 1)
            self.down(n - 2)
            self.down(n - 1)
            for (kind, j), mark in self.marks.items():
                if kind in self.places and kind != "split_gate_up_gpsimd":
                    line, place = self.places[kind]
                    assert mark[1] == self.start[line] + place(j, n), (kind, j)
            self.fold(TF.now())

        def gate_up(self, j, split):
            bank, b = banks[4 + j % 2], j % 2
            wh, wl = (x[:, b, :].rearrange("p (k n) -> p k n", k=KT) for x in (WH, WL))
            TF.wait(*split, self.at("multiplied", j - 2))
            for i in range(KT):
                last = product(bank.ap[:, 0:2 * P], HH[:, i, 0:CAP], HL[:, i, 0:CAP], wh[:, i, :], wl[:, i, :],
                               i == 0, i == KT - 1)
            made = self.marks["gate_up", j] = TF.mark(last)
            a = AF((made, self.at("multiplied", j - 2)), act_e.activation, SG[:, b, 0:P], bank.ap[:, 0:P], ACT.Silu)
            self.marks["multiplied", j] = VF((a, self.at("turned", j - 2)), vec.tensor_tensor, GC[:, b, 0:P],
                                             SG[:, b, 0:P], bank.ap[:, P:2 * P], ALU.mult)

        def turn_tile(self, j):
            b = j % 2
            to = banks[6 + b].ap[:, 0:P]
            turned = self.marks["turned", j] = TF((self.at("multiplied", j), self.tile_done(j - 2)), pe_e.transpose, to, GC[:, b, 0:P],
                                                  IDENT[:, :])
            h = AF((turned, self.down_done(j - 2)), act_e.copy, AH[:, b, 0:CAP], to)
            self.marks["tile", j] = VF((h,), vec.tensor_tensor, AL[:, b, 0:CAP], to, f32(AH[:, b, 0:CAP]),
                                       ALU.subtract)

    dense = FeedForward(Chunks(dr["all_ff"], DENSE_AT), S, Swiglu(), fold_rows(X))
    dense.begin()
    h_ready = norm_columns(X, g_dense, HT, x_ready, x_ready)
    x_ready = dense.run(FF // P, h_ready)
    ring.plan([dr["b_w_in"][c] for c in range(13)] + [dr["b_w_out"][c] for c in range(4)])


    h_ready = norm_columns(X, g_bmix, HT, x_ready, x_ready)
    used[0] = 0
    qT, kT, F_, B_ = room(HEADS, S), room(HEADS, S), room(HEADS, S), room(HEADS, S)
    v, gate, qm = room(TT, 768), room(TT, 768), room(2, S)
    QK = HT[:, 0:HEADS, :]
    AIN = room(HEADS, TT, P)
    ACR = FING[:, 0:HEADS * P].rearrange("p (h n) -> p h n", h=HEADS)
    O = XN
    mq = project(3, h_ready, copy_to(qT), "columns")

    def forget(c, seen, m):
        a = A((m,), act_e.activation, F_[:, 2 * c:2 * c + 2, :], seen, ACT.Sigmoid)
        b = A((m,), act_e.activation, kT[:, 2 * c:2 * c + 2, :], seen, ACT.Sigmoid, scale=-1.0)
        return (b,)

    mf = project(3, h_ready, forget, "columns")
    mv = project(3, h_ready, copy_rows(v), "rows")
    mg = project(3, h_ready, copy_rows(gate, func=ACT.Silu), "rows")
    mm = project(1, h_ready, copy_to(qm, HD ** -0.5), "columns")
    V.wait(lb_ready, *mf)
    for h in range(HEADS):
        V((), vec.tensor_scalar, F_[:, h, :], F_[:, h, :], OMLB[:, h:h + 1], LB[:, h:h + 1], ALU.mult, ALU.add)
        V((), vec.tensor_scalar, kT[:, h, :], kT[:, h, :], OMLB[:, h:h + 1], None, ALU.mult)
    k_ready = V.now()
    m = V((k_ready,), vec.tensor_scalar, F_[:, :, :], F_[:, :, :], 2.0 ** -63, None, ALU.max)
    m = A((m,), act_e.activation, F_[:, :, :], F_[:, :, :], ACT.Ln)
    for h in range(HEADS):
        m2 = V((m,), vec.tensor_tensor_scan, B_[:, h, :], RESET[:, :], F_[:, h, :], 0.0, ALU.mult, ALU.add)
    b_ready = m2
    zero = V((), vec.memset, AIN[:, :, :, :], 0.0)

    def halves(ap, n):
        return ap.rearrange("p h (b s n) -> p (h b) s n", s=2, n=n)

    DECAY = [F_, XN[:, :, :].rearrange("p t n -> p (t n)")[:, 0:HEADS * S].rearrange("p (h n) -> p h n", h=HEADS)]

    def decays(lv, read):
        n = 1 << lv
        to = DECAY[lv % 2]
        E, B4 = halves(to, n), halves(B_, n)
        mid = B4[:, :, 0, n - 1:n].broadcast_to([P, B4.shape[1], n])
        V.wait(b_ready, read)
        V((), vec.tensor_tensor, E[:, :, 0, :], mid, B4[:, :, 0, :], ALU.subtract)
        if n < CH:
            m = V((), vec.tensor_tensor, E[:, :, 1, :], B4[:, :, 1, :], mid, ALU.subtract)
        else:
            m = V((), vec.tensor_copy, E[:, :, 1, :], B4[:, :, 1, :])
        return A((m,), act_e.activation, to, to, ACT.Exp)

    def level_products(lhs, rhs, ready):
        made = []
        for h0 in range(0, HEADS, 2):
            bank = next_bank()
            T.wait(ready, *bank.free)
            for h in (h0, h0 + 1):
                for t in range(TT):
                    c = ((h - h0) * TT + t) * P
                    cut = slice(t * P, (t + 1) * P)
                    last = pe_e.matmul(bank.ap[:, c:c + P], lhs[:, h, cut], rhs[:, h, cut], start=True, stop=True)
            made.append((h0, bank, T.mark(last)))
        return made

    def mask_level(made, mask):
        for h0, bank, m in made:
            into = AIN[:, h0:h0 + 2, :, :].rearrange("p h t n -> p (h t) n")
            seen = bank.ap.rearrange("p (a n) -> p a n", n=P)
            m = V((m, zero), vec.copy_predicated, into, mask.unsqueeze(1).broadcast_to([P, 4, P]), seen)
            bank.free = (m,)

    made, mask = level_products(kT, qT, k_ready), LEVEL[:, 7, :]
    read = [b_ready, b_ready]
    decayed = decays(0, read[0])
    for lv in range(7):
        here = decayed
        if lv < 6:
            decayed = decays(lv + 1, read[(lv + 1) % 2])
        mask_level(made, mask)
        n = 1 << lv
        E, Q4 = halves(DECAY[lv % 2], n), halves(QK, n)
        V.wait(here, T.now())
        V((), vec.tensor_tensor, Q4[:, :, 0, :], E[:, :, 0, :], halves(kT, n)[:, :, 0, :], ALU.mult)
        m = V((), vec.tensor_tensor, Q4[:, :, 1, :], E[:, :, 1, :], halves(qT, n)[:, :, 1, :], ALU.mult)
        read[lv % 2] = m
        made, mask = level_products(QK, QK, m), LEVEL[:, lv, :]
    exps_read = m
    ends = [B_[:, :, (c + 1) * CH - 1:(c + 1) * CH] for c in range(4)]
    def chunk(ap, c):
        return ap[:, :, c * CH:(c + 1) * CH]
    def wide(ap):
        return ap.broadcast_to([P, HEADS, CH])
    V.wait(exps_read)
    m = V((), vec.tensor_tensor, chunk(F_, 0), wide(ends[0]), chunk(B_, 0), ALU.subtract)
    V((m,), vec.tensor_tensor, chunk(F_, 0), chunk(F_, 0), wide(ends[1]), ALU.add)
    V((), vec.tensor_tensor, chunk(F_, 1), wide(ends[1]), chunk(B_, 1), ALU.subtract)
    V((), vec.tensor_copy, chunk(F_, 2), chunk(B_, 2))
    m = V((), vec.tensor_tensor, chunk(F_, 3), chunk(B_, 3), wide(ends[2]), ALU.add)
    m = A((m,), act_e.activation, F_[:, :, :], F_[:, :, :], ACT.Exp)
    mask_level(made, mask)
    V.wait(m, T.now())
    V((), vec.tensor_tensor, QK[:, :, 0:P], F_[:, :, 0:P], kT[:, :, 0:P], ALU.mult)
    m = V((), vec.tensor_tensor, QK[:, :, P:S], F_[:, :, P:S], qT[:, :, P:S], ALU.mult)
    for h0 in (0, 4):
        bank = next_bank()
        T.wait(m, *bank.free)
        w = min(4, HEADS - h0)
        for h in range(h0, h0 + w):
            last = pe_e.matmul(bank.ap[:, (h - h0) * P:(h - h0 + 1) * P], QK[:, h, 0:P], QK[:, h, P:S], start=True,
                               stop=True)
        mc = T.mark(last)
        bank.free = (A((mc,), act_e.copy, ACR[:, h0:h0 + w, :],
                       bank.ap[:, 0:w * P].rearrange("p (h n) -> p h n", h=w)),)
    a_ready = (V.now(), A.now())
    for t in range(TT):
        for h0 in (0, 4):
            bank = next_bank()
            w = min(4, HEADS - h0)
            T.wait(*a_ready, *mv, *bank.free)
            for h in range(h0, h0 + w):
                to = bank.ap[:, (h - h0) * P:(h - h0 + 1) * P]
                last = pe_e.matmul(to, AIN[:, h, t, :], v[:, t, h * P:(h + 1) * P], start=True, stop=t == 0)
                if t:
                    last = pe_e.matmul(to, ACR[:, h, :], v[:, 0, h * P:(h + 1) * P], start=False, stop=True)
            mo = T.mark(last)
            bank.free = (A((mo,), act_e.copy, O[:, t, h0 * P:(h0 + w) * P], bank.ap[:, 0:w * P]),)
    heads = O[:, :, 0:768]
    ssq = stat(TT * HEADS)
    SQ = QK.rearrange("p h n -> p (h n)").rearrange("p (t n) -> p t n", t=TT)
    m = A((A.now(), T.now()), act_e.activation, SQ, heads, ACT.Square)
    m = V((m,), vec.tensor_reduce, ssq.rearrange("p (t h) -> p t h", t=TT),
          SQ.rearrange("p t (h e) -> p t h e", h=HEADS), AX_X, ALU.add)
    r = root(ssq, 12, P, (m,))
    for t in range(TT):
        part = heads[:, t, :].rearrange("p (h e) -> p h e", h=HEADS)
        m = V((r,), vec.tensor_tensor, part, part, spread(ssq[:, t * HEADS:(t + 1) * HEADS], P), ALU.mult)
    gated = V((m, *mg), vec.tensor_tensor, heads, heads, gate[:, :, :], ALU.mult)
    p_bufs = [QK.rearrange("p h n -> p (h n)")[:, 0:512].unsqueeze(1), QK.rearrange("p h n -> p (h n)")[:, 512:1024].unsqueeze(1)], \
        [AIN.rearrange("p h t n -> p (h t n)")[:, 0:512], AIN.rearrange("p h t n -> p (h t n)")[:, 512:1024]]
    for q in (V, A, T):
        q.wait(gated, T.now(), A.now())
    done = mixer_memory(KVB[:, :, :], qm, O, mm, p_bufs)
    o_ready = turn(lambda t, c: O[:, t, c * P:(c + 1) * P], KT, GB, HT, (*done, gated), (T.now(), A.now(), V.now()))
    x_ready = project(4, o_ready, add_rows(X), "rows")



    A.wait(*x_ready, V.now())
    layer_in.mark(act_e.dma_start(FING[:], dr["final_norm"].broadcast_to([P, D])))
    used[0] = 0
    PICK, PICKT, YA, HE = room(TT, CAP), room(TT, P), room(D), room(KT, CAP)
    SEL, RANK, COMB = room(TT, NE + 1), room(TT, NE + 1), room(TT, NE + 1)
    SHIFT = room(TT)
    COUNT = sb("expert_counts", [P, NE + 1], I32)

    def fold_expert(m):
        VF((m,), vec.tensor_tensor, YA, YA, PS[:, 0:2, :].rearrange("p a b -> p (a b)"), ALU.add)
    fold_expert.ops = 1

    experts = GatheredFeedForward(Chunks(dr["all_ff"], 0), fold_expert)
    experts.begin()
    h_ready = norm_columns(X, g_moe, HT, x_ready, x_ready)
    lg, top8, hot, hot2, idxf, w12 = stat(TT * NE), stat(8), stat(NE), stat(NE), stat(2), stat(4)
    clear = V((), vec.memset, SEL, 0.0)
    clear = V((), vec.memset, COMB, 0.0)
    clear = V((), vec.memset, RANK, 0.0)
    for t in range(TT):
        bank = banks[t]
        T.wait(*h_ready, *bank.free)
        for i in range(KT):
            last = pe_e.matmul(bank.ap[:, 0:NE], HT[:, i, t * P:(t + 1) * P], ROUT[:, i, :], start=i == 0,
                               stop=i == KT - 1)
        m = T.mark(last)
        mine = lg[:, t * NE:(t + 1) * NE]
        m = V((m,), vec.tensor_copy, mine, bank.ap[:, 0:NE])
        bank.free = (m,)
        m = V((m,), vec.max, top8, mine)
        m = V((m,), vec.max_index, STI[:, 0:8], top8, mine)
        m = V((m,), vec.tensor_copy, idxf, STI[:, 0:2])
        m = V((m,), vec.tensor_tensor, w12[:, 0:1], top8[:, 1:2], top8[:, 0:1], ALU.subtract)
        e = A((m,), act_e.activation, w12[:, 1:2], w12[:, 0:1], ACT.Exp)
        m = V((e,), vec.tensor_scalar, w12[:, 2:3], w12[:, 1:2], 1.0, None, ALU.add)
        m = V((m,), vec.reciprocal, w12[:, 2:3], w12[:, 2:3])
        m = V((m,), vec.tensor_tensor, w12[:, 3:4], w12[:, 1:2], w12[:, 2:3], ALU.mult)
        V((m,), vec.tensor_scalar, hot, IOTA[:, :], idxf[:, 0:1], None, ALU.is_equal)
        m = V((), vec.tensor_scalar, hot2, IOTA[:, :], idxf[:, 1:2], None, ALU.is_equal)
        V((m, clear), vec.tensor_tensor, SEL[:, t, 0:NE], hot, hot2, ALU.add)
        m = V((), vec.tensor_scalar, hot, hot, w12[:, 2:3], None, ALU.mult)
        m = V((m,), vec.scalar_tensor_tensor, COMB[:, t, 0:NE], hot2, w12[:, 3:4], hot, ALU.mult, ALU.add)
        V.wait(m)
    T.wait(m, *banks[2].free, *banks[3].free)
    for t in range(TT):
        last = pe_e.matmul(banks[2].ap[:, t * NE:(t + 1) * NE], TRIL[:, :], SEL[:, t, 0:NE], start=True, stop=t == 0)
        if t:
            last = pe_e.matmul(banks[2].ap[:, t * NE:(t + 1) * NE], ONES[:, :], SEL[:, 0, 0:NE], start=False,
                               stop=True)
    for t in range(TT):
        last = pe_e.matmul(banks[3].ap[:, 0:NE], ONES[:, :], SEL[:, t, 0:NE], start=t == 0, stop=t == 1)
    m = T.mark(last)
    V((m,), vec.tensor_copy, RANK[:, :, 0:NE], banks[2].ap[:, 0:TT * NE].rearrange("p (t n) -> p t n", t=TT))
    V((), vec.tensor_copy, COUNT[:, 0:NE], banks[3].ap[:, 0:NE])
    top = stat(1)
    m = V((), vec.tensor_reduce, top, banks[3].ap[:, 0:NE], AX_X, ALU.max)
    ranked = V((m,), vec.tensor_copy, COUNT[:, NE:NE + 1], top)
    banks[2].free = banks[3].free = (ranked,)

    def pick(e, rank, free):
        V.wait(*free)
        for t in range(TT):
            m = V((), vec.tensor_scalar, PICK[:, t, :], PLACE[:, :], rank(t), SEL[:, t, bass.ds(e, 1)],
                  ALU.is_equal, ALU.mult)
        return m

    def gather(picked):
        for b in range(2):
            bank = banks[2 + b]
            T.wait(picked, *bank.free)
            for c in range(4):
                for t in range(TT):
                    last = pe_e.matmul(bank.ap[:, c * CAP:(c + 1) * CAP], XN[:, t, (4 * b + c) * P:(4 * b + c + 1) * P],
                                       PICK[:, t, :], start=t == 0, stop=t == 1)
            m = T.mark(last)
            part = slice(4 * b, 4 * b + 4)
            m = VG((m,), vec.tensor_tensor, HE[:, part, :], bank.ap.rearrange("p (c n) -> p c n", c=4),
                   spread(g_moe[:, part], CAP), ALU.mult)
            bank.free = (m,)
            h = A((m, TF.now()), act_e.copy, HH[:, part, 0:CAP], HE[:, part, :])
            VG((h, TF.now()), vec.tensor_tensor, HL[:, part, 0:CAP], HE[:, part, :], f32(HH[:, part, 0:CAP]),
               ALU.subtract)

    def turn_pick(picked):
        T.wait(picked, *banks[6].free)
        for t in range(TT):
            last = pe_e.transpose(banks[6].ap[:, t * P:(t + 1) * P], PICK[:, t, :], IDENT[:, :])
        m = T.mark(last)
        banks[6].free = (A((m, T.now()), act_e.copy, PICKT, banks[6].ap[:, 0:TT * P].rearrange("p (t n) -> p t n", t=TT)),)

    def scatter(e, pick_turned):
        T.wait(VF.now(), pick_turned)
        for k, (t, h) in enumerate(((0, 0), (0, 1), (1, 0), (1, 1))):
            bank = banks[(6, 2, 3, 7)[k]]
            T.wait(*bank.free)
            m = T((), pe_e.matmul, bank.ap, PICKT[:, t, :], YA[:, h * 512:(h + 1) * 512], start=True, stop=True)
            part = X[:, t, h * 512:(h + 1) * 512]
            bank.free = (V((m,), vec.scalar_tensor_tensor, part, bank.ap, COMB[:, t, bass.ds(e, 1)], part, ALU.mult,
                           ALU.add),)

    def empty_sum():
        return V((T.now(),), vec.memset, YA, 0.0)

    TF.wait(ranked)
    for b in banks:
        TF.wait(*b.free)
        V.wait(*b.free)
    picked = pick(0, lambda t: RANK[:, t, 0:1], (ranked,))
    gather(picked)
    turn_pick(picked)
    once = {T: 7, V: 7, VG: 4, A: 3}
    with Turns(nc, NE, lines, {**once, **experts.expert_counts()}) as e:
        for b in banks:
            b.free = ()
        TF.wait(VG.now())
        pick_turned = A.now()
        VF.wait(empty_sum())
        picked = pick(e + 1, lambda t: RANK[:, t, bass.ds(e + 1, 1)], (T.now(),))
        experts.expert(e * ETILES)
        gather(picked)
        scatter(e, pick_turned)
        turn_pick(picked)

    A.wait(down_slots[0].now())
    V.wait(layer_in.now())
    nc.all_engine_barrier()
    with nc.If(nc.values_load(COUNT[0:1, NE:NE + 1], min_val=0, max_val=S) > CAP):
        with nc.Fori(0, NE) as e:
            with nc.If(nc.values_load(COUNT[0:1, bass.ds(e, 1)], min_val=0, max_val=S) > CAP):
                start_anew()
                experts.begin(e * ETILES)
                for t in range(TT):
                    m = V((), vec.tensor_scalar, SHIFT[:, t:t + 1], RANK[:, t, bass.ds(e, 1)], float(-CAP), None, ALU.add)
                picked = pick(e, lambda t: SHIFT[:, t:t + 1], (m,))
                gather(picked)
                turn_pick(picked)
                TF.wait(VG.now())
                VF.wait(empty_sum())
                experts.expert(e * ETILES)
                scatter(e, A.now())
                SP.wait(VS.now(), GS.now())
                A.wait(down_slots[0].now())
    start_anew()

    m = rms_scale(X, XN, D, (), ())
    for t in range(TT):
        m2 = V(m, vec.tensor_tensor, X[:, t, :], XN[:, t, :], FING[:, :], ALU.mult)

    NL = 2
    PL = sb("layer_columns", [P, 536])
    B2 = sb("compressed_bias", [NC, 2, HD])
    with nc.Fori(0, NL) as layer:
        start_anew()

        def of_layer(name, c=0, n=1):
            return dr[name][bass.ds(layer * n + c, 1)].rearrange("o p n -> (o p) n")

        used[0] = 0
        ZQK, ZV, ZC = room(TT, 768), room(TT, 256), room(TT, 256)
        SPARE = XN[:, :, :].rearrange("p a b -> p (a b)")
        ZD = SPARE[:, 0:1024].rearrange("p (a b) -> p a b", a=TT)
        ZT = SPARE[:, 1024:2048].rearrange("p (a b) -> p a b", a=4)
        FL, HC = room(2, GROUPS * NC, PAIRS), room(2, 2, GROUPS * NC)
        KVC, KCT, QKT = room(4 * HD)[0:NC], room(NC), room(6, S)
        MX, VV, WS, LN = room(TT, D), room(TT, 512), room(8, P), room(2, 512)
        GT = room(TT, GW)
        CV = ARENA[:, 0:512].rearrange("p (a b) -> p a b", a=2)
        PLT = ARENA[:, 512:1024].rearrange("p (a b) -> p a b", a=2)
        buf = [SPARE[:, 512 * i:512 * (i + 1)] for i in range(4)]
        p_bufs = [buf[0].unsqueeze(1), buf[1].unsqueeze(1)], [buf[2], buf[3]]

        columns_in.mark(act_e.dma_start(PL[:, :], of_layer("layer_columns")))
        ring.plan([of_layer("w_in", c, 9) for c in range(9)])
        ring.plan([of_layer("cmp_w1", c, 4) for c in range(4)], raw=True)
        ring.plan([of_layer("w_o", c, 4) for c in range(4)])
        g_pre, g_ffn, g_ple, g_mix = (PL[:, 8 * i:8 * i + 8] for i in range(4))
        b1 = PL[:, 32:36]
        bs = PL[:, 36:44]
        wg = PL[:, 44:236].rearrange("p (k n) -> p k n", k=KT)
        pe_col = PL[:, 236:268].rearrange("p (k n) -> p k n", k=2)
        w2 = PL[:, 268:524].rearrange("p (k h n) -> p k h n", k=2, h=2)

        h_ready = norm_columns(X, g_pre, HT, (), (columns_in.now(),))
        for q in (V, A, T):
            q.wait(columns_in.now())
        for dst, src in ((B2[:, :, :].rearrange("p a b -> p (a b)"), of_layer("cmp_b2").broadcast_to([NC, 2 * HD])),
                         (WS.rearrange("p a b -> p (a b)"), of_layer("gmlp_ws")),
                         (LN.rearrange("p a b -> p (a b)"), of_layer("gmlp_ln").broadcast_to([P, D])),
                         (FING[:, :], of_layer("post_mix_g").broadcast_to([P, D]))):
            layer_in.mark(act_e.dma_start(dst, src))

        def evac_qk(c, seen, m):
            return (A((m,), act_e.activation, ZQK[:, :, c * 256:(c + 1) * 256], seen, ACT.Copy,
                      scale=HD ** -0.5 if c < 2 else 1.0),)

        mqk = project(3, h_ready, evac_qk, "rows")
        mv = project(1, h_ready, copy_rows(ZV), "rows")
        mc = project(1, h_ready, copy_rows(ZC), "rows")

        def rope(z, cs, heads, ready):
            n = z.shape[0]
            x1, x2 = z[:, :, 0:8], z[:, :, 8:16]
            cos = cs[:, 0:8].unsqueeze(1).broadcast_to([n, heads, 8])
            sin = cs[:, 8:16].unsqueeze(1).broadcast_to([n, heads, 8])
            tmp = RT[0:n].rearrange("p (k h n) -> p k h n", k=4, h=12)[:, :, 0:heads, :]
            V.wait(V.now())
            V(ready, vec.tensor_tensor, tmp[:, 0], x1, cos, ALU.mult)
            V((), vec.tensor_tensor, tmp[:, 1], x2, sin, ALU.mult)
            V((), vec.tensor_tensor, tmp[:, 2], x2, cos, ALU.mult)
            m = V((), vec.tensor_tensor, tmp[:, 3], x1, sin, ALU.mult)
            V((m,), vec.tensor_tensor, x1, tmp[:, 0], tmp[:, 1], ALU.subtract)
            return V((), vec.tensor_tensor, x2, tmp[:, 2], tmp[:, 3], ALU.add)

        RT = VV[:, 0, 0:384]
        for t in range(TT):
            rm = rope(ZQK[:, t, :].rearrange("p (h d) -> p h d", h=12), ROPE[:, t, :], 12, mqk)
        qk_ready = turn(lambda t, c: ZQK[:, t, c * P:(c + 1) * P], 6, None, QKT, (rm,))
        for t in range(TT):
            dup = A((*mc, T.now()), act_e.copy, ZD[:, t, :].rearrange("p (g u d) -> p g u d", g=4, u=2),
                    ZC[:, t, :].rearrange("p (g d) -> p g d", g=4).unsqueeze(2).broadcast_to([P, 4, 2, HD]))
        c_ready = turn(lambda t, c: ZD[:, t, c * P:(c + 1) * P], 4, None, ZT, (dup,))
        V.wait(*c_ready)
        Z16 = ZT.rearrange("p g (n l) -> p g n l", l=CSTR)
        F16 = FL.rearrange("p k (g n) j -> p k g n j", g=GROUPS)
        for kv in range(2):
            for odd in range(2):
                for late in range(2):
                    rows_ = half(odd)
                    V((), vec.tensor_tensor, F16[rows_, kv, :, :, 8 * late:8 * late + 8],
                      Z16[rows_, 2 * kv:2 * kv + 2, late:late + NC, odd:CSTR:2],
                      pe_col[rows_, kv, 8 * late:8 * late + 8].unsqueeze(1).unsqueeze(1)
                      .broadcast_to([64, GROUPS, NC, 8]), ALU.add)
        blocks_ready = V.now()

        bank = next_bank()
        T.wait(*h_ready, *bank.free)
        for t in range(TT):
            for i in range(KT):
                last = pe_e.matmul(bank.ap[:, t * GW:(t + 1) * GW], HT[:, i, t * P:(t + 1) * P], wg[:, i, :],
                                   start=i == 0, stop=i == KT - 1)
        m = T.mark(last)
        gates = A((m,), act_e.activation, GT, bank.ap[:, 0:TT * GW].rearrange("p (t n) -> p t n", t=TT), ACT.Sigmoid)
        bank.free = (gates,)
        mu = project(2, h_ready, copy_rows(MX[:, :, 512:D], func=ACT.Gelu_apprx_tanh), "rows")
        A.wait(rm)
        mvv = project(2, h_ready, copy_rows(VV, func=ACT.Gelu_apprx_tanh), "rows")

        V.wait(layer_in.now())
        wsm = V((), vec.tensor_tensor, WS, WS, TRIL[:, :].unsqueeze(1).broadcast_to([P, 8, P]), ALU.mult)
        V.wait(*mvv)
        bn, mv2 = stat(12), stat(4)
        for t in range(TT):
            m = V((), vec.bn_stats, bn[:, 6 * t:6 * t + 6], VV[:, t, :])
            m = V((m,), vec.bn_aggr, mv2[:, 2 * t:2 * t + 2], bn[:, 6 * t:6 * t + 6])
            m = V((m,), vec.tensor_scalar, mv2[:, 2 * t + 1:2 * t + 2], mv2[:, 2 * t + 1:2 * t + 2], EPS, None, ALU.add)
            m = A((m,), act_e.activation, mv2[:, 2 * t + 1:2 * t + 2], mv2[:, 2 * t + 1:2 * t + 2], ACT.Sqrt)
            m = V((m,), vec.reciprocal, mv2[:, 2 * t + 1:2 * t + 2], mv2[:, 2 * t + 1:2 * t + 2])
            m = V((m,), vec.tensor_scalar, VV[:, t, :], VV[:, t, :], mv2[:, 2 * t:2 * t + 1],
                  mv2[:, 2 * t + 1:2 * t + 2], ALU.subtract, ALU.mult)
            m = V((m,), vec.tensor_tensor, VV[:, t, :], VV[:, t, :], LN[:, 0, :], ALU.mult)
            ln = V((m,), vec.tensor_tensor, VV[:, t, :], VV[:, t, :], LN[:, 1, :], ALU.add)

        for kv in range(2):
            pair = banks[2 * kv], banks[2 * kv + 1]
            T.wait(blocks_ready, *pair[0].free, *pair[1].free)
            for part in range(2):
                w, arrived = ring.take_raw()
                w = w[:, 0:8 * 256].rearrange("p (k n) -> p k n", k=8)
                T.wait(arrived)
                for hid in range(2):
                    for j in range(8):
                        last = pe_e.matmul(pair[hid].ap[:, 0:GROUPS * NC], w[:, j, hid * P:(hid + 1) * P],
                                           FL[:, kv, :, 8 * part + j], start=part == 0 and j == 0,
                                           stop=part == 1 and j == 7)
                m = T.mark(last)
                ring.taken_raw_by(m)
            for hid in range(2):
                a = A((m,), act_e.activation, HC[:, kv, hid, :], pair[hid].ap[:, 0:GROUPS * NC],
                      ACT.Gelu_apprx_tanh, bias=b1[:, 2 * kv + hid:2 * kv + hid + 1])
                pair[hid].free = (a,)
        bank = next_bank()
        T.wait(a, *bank.free)
        for kv in range(2):
            for g in range(GROUPS):
                c = (kv * GROUPS + g) * HD
                for hid in range(2):
                    last = pe_e.matmul(bank.ap[0:NC, c:c + HD], HC[:, kv, hid, g * NC:(g + 1) * NC],
                                       w2[:, kv, hid, :], start=hid == 0, stop=hid == 1)
        m = T.mark(last)
        kvc = KVC.rearrange("p (k g d) -> p k g d", k=2, g=GROUPS)
        m = V((m,), vec.tensor_tensor, kvc, bank.ap[0:NC, 0:256].rearrange("p (k g d) -> p k g d", k=2, g=GROUPS),
              B2[:, :, :].unsqueeze(2).broadcast_to([NC, 2, GROUPS, HD]), ALU.add)
        bank.free = (m,)
        RT = HT[:, 0:2, :].rearrange("p a b -> p (a b)")[:, 0:384]
        m = rope(kvc[:, 0], CROPE[:, :], GROUPS, (m,))
        bank = next_bank()
        T.wait(*bank.free)
        m = T((m,), pe_e.transpose, bank.ap[:, 0:NC], KVC[:, 0:GROUPS * HD], IDENT[0:NC, 0:NC])
        kct_ready = V((m,), vec.tensor_copy, KCT, bank.ap[:, 0:NC])
        bank.free = (kct_ready,)

        V.wait(*mu)
        for t in range(TT):
            bank = next_bank()
            T.wait(ln, wsm, *bank.free)
            for g in range(8):
                last = pe_e.matmul(bank.ap[:, g * HD:(g + 1) * HD], WS[:, g, :], VV[:, t, g * HD:(g + 1) * HD],
                                   start=True, stop=True)
            m = T.mark(last)
            m = V((m,), vec.tensor_tensor, VV[:, t, :].rearrange("p (g d) -> p g d", g=8),
                  bank.ap.rearrange("p (g d) -> p g d", g=8), spread(bs, HD), ALU.add)
            bank.free = (m,)
            mlp = V((m,), vec.tensor_tensor, MX[:, t, 512:D], MX[:, t, 512:D], VV[:, t, :], ALU.mult)

        def add_mask(mask):
            def go(h, mine, raw, ready):
                return V(ready, vec.tensor_tensor, mine, raw, mask, ALU.add)
            return go

        V.wait(gates)

        def branch(br):
            def finish(h, seen, tot, m):
                o = MX[:, :, h * HD:(h + 1) * HD]
                w = stat(TT)
                g = V((m,), vec.tensor_tensor, w, tot, GT[:, :, 3 * h + br], ALU.mult)
                if br == 0:
                    return V((g,), vec.tensor_tensor, o, seen, spread(w, HD), ALU.mult)
                for t in range(TT):
                    g = V((g,), vec.scalar_tensor_tensor, o[:, t, :], seen[:, t, :], w[:, t:t + 1], o[:, t, :],
                          ALU.mult, ALU.add)
                return g
            return finish

        def query(h, m, q):
            return QKT[half(h // 4), h % 4, q * P:(q + 1) * P]

        cmp_segs = [(0, NC, 0), (1, NC, NC)]
        attend(NH2, cmp_segs, query, lambda h, m, n: KCT[half(h // 4), :],
               lambda h, i: KVC[:, (GROUPS + h // 4) * HD:(GROUPS + h // 4 + 1) * HD],
               add_mask(CMPA[:, :, :].rearrange("p t n -> p (t n)")), branch(0), (*qk_ready, kct_ready), p_bufs, HD,
               keys=NC, keep=CMPK[:, :, :].rearrange("p t n -> p (t n)"))
        def value(hh, i):
            c = (hh // NH2 * GROUPS + hh % NH2 // 4) * HD
            return ZV[:, i, c:c + HD]

        finishers = branch(1), branch(2)
        done = attend(2 * NH2, TRI, lambda hh, m, q: query(hh % NH2, m, q),
                      lambda hh, m, n: QKT[half(hh % NH2 // 4), 4 + hh // NH2, 0:n], value, add_mask(CAUS[:, :]),
                      lambda hh, *args: finishers[hh // NH2](hh % NH2, *args), (*qk_ready, *mv, V.now(), A.now()),
                      p_bufs, HD)

        ssq = stat(4)
        A.wait(*done, mlp, T.now())
        for t in range(TT):
            for s in range(2):
                m = A((), act_e.activation, XN[:, t, s * 512:(s + 1) * 512], MX[:, t, s * 512:(s + 1) * 512],
                      ACT.Square, accum_out=ssq[:, 2 * t + s:2 * t + s + 1])
        r = root(ssq, 4, 512, (m,))
        for t in range(TT):
            for s in range(2):
                m = A((r,), act_e.activation, MX[:, t, s * 512:(s + 1) * 512], MX[:, t, s * 512:(s + 1) * 512],
                      ACT.Copy, scale=ssq[:, 2 * t + s:2 * t + s + 1])
        mix_ready = turn(lambda t, c: MX[:, t, c * P:(c + 1) * P], KT, g_mix, HT, (m,), (T.now(),))
        made = project(4, mix_ready, copy_rows(XN), "rows")

        def add_normed(gain, ready):
            m = rms_scale(XN, MX, D, ready, (T.now(), V.now()))
            for t in range(TT):
                v = V((m[t],), vec.tensor_tensor, MX[:, t, :], MX[:, t, :], gain, ALU.mult)
                v = V((v,), vec.tensor_tensor, X[:, t, :], X[:, t, :], MX[:, t, :], ALU.add)
            return v

        x_ready = add_normed(FING[:, :], made)

        A.wait(x_ready)
        layer_in.mark(act_e.dma_start(FING[:, :], of_layer("post_ffn_g").broadcast_to([P, D])))
        layer_in.mark(act_e.dma_start(PLT.rearrange("p a b -> p (a b)"), of_layer("p_columns")))
        conv = FeedForward(Chunks(dr["conv_ff"], layer * (FF // P), SLOT), S, Conv(), fold_rows(XN))
        conv.begin()
        h_ready = norm_columns(X, g_ffn, HT, (x_ready,), (x_ready,))
        zero = V((*h_ready, T.now()), vec.memset, XN[:, :, :], 0.0)
        done = conv.run(FF // P, (*h_ready, zero))
        ring.plan([of_layer("w_ple_proj")], raw=True)
        ring.plan([of_layer("w_ple_gate", c, 4) for c in range(4)])
        V.wait(layer_in.now())
        x_ready = add_normed(FING[:, :], done)

        w, arrived = ring.take_raw()
        w = w[:, 0:2 * D].rearrange("p (k n) -> p k n", k=2)
        T.wait(arrived, layer_in.now())
        for b in banks[0:4]:
            T.wait(*b.free)
        for t in range(TT):
            for s in range(2):
                for i in range(2):
                    last = pe_e.matmul(banks[2 * t + s].ap, PLT[:, i, t * P:(t + 1) * P],
                                       w[:, i, s * 512:(s + 1) * 512], start=i == 0, stop=i == 1)
        ple = T.mark(last)
        ring.taken_raw_by(ple)
        h_ready = norm_columns(X, g_ple, HT, (x_ready,), (x_ready,))
        gm = project(4, h_ready, copy_rows(MX, func=ACT.Sigmoid), "rows")
        for t in range(TT):
            v = V((*gm, ple), vec.tensor_tensor, MX[:, t, :], MX[:, t, :],
                  PS[:, 2 * t:2 * t + 2, :].rearrange("p a b -> p (a b)"), ALU.mult)
            v = V((v,), vec.tensor_tensor, X[:, t, :], X[:, t, :], MX[:, t, :], ALU.add)

    stored.mark(sync_wait_store(SP, (V.now(),), sync, out, X))
    sync.wait_ge(stored.sem, stored.count)


def sync_wait_store(SP, ready, sync, out, X):
    SP.wait(*ready)
    return sync.dma_start(out, X[:])


def constants():
    f = np.float32
    c = {"ident": np.eye(P, dtype=f)}
    q, k = np.arange(S)[:, None], np.arange(S)[None, :]

    def tri(a):
        return np.concatenate([a[0:P, 0:P], a[P:S, :]], axis=1).astype(f)

    c["dist"] = tri(np.where(k // CH <= q // CH, np.abs(q - k), FAR))
    c["causal"] = tri(np.where(k <= q, 0.0, NEG))
    s, t = np.arange(P)[:, None], np.arange(P)[None, :]
    levels = [((s // (2 * n) == t // (2 * n)) & (s // n % 2 == 0) & (t // n % 2 == 1)) for n in (1 << lv for lv in range(7))]
    c["levels"] = np.stack(levels + [s == t], axis=1).astype(np.int32)
    c["reset"] = np.broadcast_to((np.arange(S) % CH != 0).astype(f), (P, S)).copy()
    c["tri"] = (s <= t).astype(f)
    inv = f(500000.0) ** (-np.arange(8, dtype=f) / f(8))

    def rope(pos):
        ang = pos.astype(f)[:, None] * inv[None, :]
        return np.concatenate([np.cos(ang), np.sin(ang)], axis=1).astype(f)

    c["rope"] = rope(np.arange(S)).reshape(TT, P, 16).transpose(1, 0, 2).copy()
    c["crope"] = rope(np.arange(NC) * CSTR + 31)
    ok = (np.arange(NC) * CSTR + 31)[None, :] <= np.arange(S)[:, None]
    c["cmp_add"] = np.where(ok, 0.0, NEG).astype(f).reshape(TT, P, NC).transpose(1, 0, 2).copy()
    c["cmp_keep"] = ok.astype(f).reshape(TT, P, NC).transpose(1, 0, 2).copy()
    c["place"] = np.broadcast_to(np.arange(1, CAP + 1, dtype=f), (P, CAP)).copy()
    c["iota"] = np.broadcast_to(np.arange(NE, dtype=f), (P, NE)).copy()
    return c


def chunked(w, n=256):
    K, N = w.shape
    return w.reshape(K // P, P, N // n, n).transpose(2, 1, 0, 3).reshape(N // n, P, K // P * n)


def columns(g):
    return g.reshape(-1, P).T


def rows(a):
    return a.reshape(TT, P, -1).transpose(1, 0, 2)


def ff_chunks(gate_up, down, extra=None):
    F = down.shape[0]
    gu = gate_up.reshape(KT, P, 2, F // P, P).transpose(3, 1, 0, 2, 4).reshape(F // P, P, 2 * D)
    parts = [gu, down.reshape(F // P, P, D)]
    if extra is not None:
        parts.append(extra)
    return np.concatenate(parts, axis=2)


def lay_out(a):
    L = {"x": rows(a["x"][0]), "mem": rows(a["mem"][0])}
    L["a_w_in"] = chunked(a["a_w_in"][0])
    L["a_w_mem_kv"] = chunked(a["a_w_mem_kv"][0])
    L["a_w_out"] = chunked(a["a_w_out"][0])
    L["b_w_in"] = chunked(a["b_w_in"][0])
    L["b_w_mem_kv"] = chunked(a["b_w_mem_kv"][0])
    L["b_w_out"] = chunked(a["b_w_out"][0])
    L["all_ff"] = np.concatenate([ff_chunks(a["moe_w_gate_up"][0, e], a["moe_w_down"][0, e]) for e in range(NE)]
                                 + [ff_chunks(a["dense_w_gate_up"][0], a["dense_w_down"][0])])
    L["gains"] = np.stack([columns(g) for g in (a["a_norm_mix"][0], a["a_mem_norm"][0], a["b_norm_mix"][0],
                                                a["b_mem_norm"][0], a["dense_norm"][0], a["moe_norm"][0],
                                                a["final_norm"])], axis=1)
    small = np.zeros((P, 10), np.float32)
    small[:, 0] = a["a_subln"][0]
    small[:, 1] = a["b_out_norm"][0]
    for i, n in enumerate(("a_lam_q1", "a_lam_k1", "a_lam_q2", "a_lam_k2")):
        small[0:HD, 4 + i] = a[n][0]
    L["small"] = small
    L["b_lb_logits"] = columns(a["b_lb_logits"][0])
    L["moe_router"] = a["moe_router"][0].reshape(KT, P, NE).transpose(1, 0, 2)
    L["final_norm"] = a["final_norm"].reshape(1, D)
    NLAY = a["w_in_2"].shape[0]
    w = a["w_in_2"]
    order = [0, 4, 1, 5, 2, 6, 3, 7]
    q, kc, vc, ks, vs, kw, vw, g, u, v = np.split(w, np.cumsum([512] + [P] * 6 + [GW, 512]), axis=2)
    q = np.concatenate([q[:, :, h * HD:(h + 1) * HD] for h in order], axis=2)
    w = np.concatenate([q, ks, kw, vs, vw, kc, vc, u, v], axis=2)
    L["w_in"] = np.concatenate([chunked(w[i]) for i in range(NLAY)])
    L["cmp_w1"] = np.concatenate([chunked(a["cmp_w1_2"][i, k, h * D:(h + 1) * D]) for i in range(NLAY)
                                  for k in range(2) for h in range(2)])
    L["w_o"] = np.concatenate([chunked(a["w_o_2"][i]) for i in range(NLAY)])
    L["w_ple_gate"] = np.concatenate([chunked(a["w_ple_gate_2"][i]) for i in range(NLAY)])
    L["w_ple_proj"] = a["w_ple_proj_2"].reshape(NLAY, 2, P, D).transpose(0, 2, 1, 3).reshape(NLAY, P, 2 * D)
    L["p_columns"] = a["p_2"][:, 0].reshape(NLAY, S, 2, P).transpose(0, 3, 2, 1).reshape(NLAY, P, 2 * S)
    L["gmlp_ws"] = a["gmlp_ws_2"].transpose(0, 3, 1, 2).reshape(NLAY, P, 8 * P)
    L["gmlp_ln"] = np.concatenate([a["gmlp_ln_g_2"], a["gmlp_ln_b_2"]], axis=1).reshape(NLAY, 1, D)
    L["post_mix_g"] = a["post_mix_g_2"].reshape(NLAY, 1, D)
    L["post_ffn_g"] = a["post_ffn_g_2"].reshape(NLAY, 1, D)
    L["cmp_b2"] = a["cmp_b2_2"].reshape(NLAY, 1, 2 * HD)
    cols = np.zeros((NLAY, P, 536), np.float32)
    for i in range(NLAY):
        cols[i, :, 0:8] = columns(a["pre_mix_g_2"][i])
        cols[i, :, 8:16] = columns(a["pre_ffn_g_2"][i])
        cols[i, :, 16:24] = columns(a["ple_norm_g_2"][i])
        cols[i, :, 24:28] = columns(a["attn_out_g_2"][i])
        cols[i, :, 28:32] = columns(a["mlp_out_g_2"][i])
        cols[i, :, 32:36] = columns(a["cmp_b1_2"][i].reshape(-1))
        cols[i, :, 36:44] = a["gmlp_bs_2"][i].T
        cols[i, :, 44:236] = g[i].reshape(KT, P, GW).transpose(1, 0, 2).reshape(P, KT * GW)
        cols[i, :, 236:268] = a["cmp_pe_2"][i].reshape(2, PAIRS, P).transpose(2, 0, 1).reshape(P, 2 * PAIRS)
        cols[i, :, 268:524] = a["cmp_w2_2"][i].reshape(2, 2, P, HD).transpose(2, 0, 1, 3).reshape(P, 4 * HD)
    L["layer_columns"] = cols
    conv = np.concatenate([a["conv_w_2"], a["conv_b_2"][:, None]], axis=1)
    conv = conv.reshape(NLAY, 4, 2, FF // P, P).transpose(0, 3, 4, 2, 1).reshape(NLAY, FF // P, P, 8)
    L["conv_ff"] = np.concatenate([ff_chunks(a["w_up_2"][i], a["w_down_2"][i], conv[i]) for i in range(NLAY)])
    return L


def kernel(**inputs):
    import concourse.bacc as _bacc
    from concourse.bass_utils import run_bass_kernel_spmd as _run

    nc = _bacc.Bacc("TRN2", target_bir_lowering=False, num_devices=1)
    arrays, dr = {}, {}
    for name, a in {**lay_out({k: np.asarray(v) for k, v in inputs.items()}), **constants()}.items():
        a = np.ascontiguousarray(a)
        arrays[f"in_{name}"] = a
        dr[name] = nc.dram_tensor(f"in_{name}", a.shape, mybir.dt.from_np(a.dtype), kind="ExternalInput").ap()
    out = nc.dram_tensor("out_rows", (P, TT, D), F32, kind="ExternalOutput").ap()
    program(nc, dr, out)
    r = _run(nc, [arrays], core_ids=[0])
    return r.results[0]["out_rows"].transpose(1, 0, 2).reshape(1, S, D)
```
